# Optimizing a Trainium2 kernel written in Bass

```python
import jax, jax.numpy as jnp
from jax import lax
import numpy as np

D_MODEL = 1024
BATCH = 1
SEQ = 256
DEPTH = 2

GRID_W = 64
CTX_LEN = 256
HEAD_DIM = D_MODEL // 16
N_ATT_HEADS = 6
N_ATT_KV = 2
N_NA_HEADS = 4
N_RET_HEADS = 6
ATT_Q = N_ATT_HEADS * HEAD_DIM
ATT_KV = N_ATT_KV * HEAD_DIM
NA_W = N_NA_HEADS * HEAD_DIM
RET_W = N_RET_HEADS * HEAD_DIM
MIX_W = ATT_Q + NA_W + RET_W
IN_COLS = ATT_Q + 2 * ATT_KV + 3 * NA_W + 4 * RET_W
Q_BLOCK = 128
NA_WIN_ROWS = 8
NA_WIN_COLS = 16
RET_CHUNK = 128
ROPE_THETA = 10000.0
N_EXPERTS = 16
N_EXPERT_GROUPS = 4
TOP_GROUPS = 1
TOP_K = 2
D_EXPERT = 512
EPS = 1e-6
NEG_INF = -1e30

kernel_name = 'hybrid_diffusion_trunk'

def _rms(x, g):
    xf = x.astype(jnp.float32)
    y = xf * lax.rsqrt(jnp.mean(xf * xf, axis=-1, keepdims=True) + EPS)
    return (y * g.astype(jnp.float32)).astype(x.dtype)

def _heads(t, n_heads):
    b, n, _ = t.shape
    return t.reshape(b, n, n_heads, HEAD_DIM).transpose(0, 2, 1, 3)

def _flat(o):
    b, h, n, d = o.shape
    return o.transpose(0, 2, 1, 3).reshape(b, n, h * d)

def _head_norm(y, g):
    b, n, w = y.shape
    hh = w // HEAD_DIM
    return _rms(y.reshape(b, n, hh, HEAD_DIM), g.reshape(hh, HEAD_DIM)).reshape(b, n, w)

def _axial_angles(n):
    t = jnp.arange(n, dtype=jnp.int32)
    row = (t // GRID_W).astype(jnp.float32)
    col = (t % GRID_W).astype(jnp.float32)
    nf = HEAD_DIM // 4
    inv = ROPE_THETA ** (-jnp.arange(nf, dtype=jnp.float32) / nf)
    return row[:, None] * inv[None, :], col[:, None] * inv[None, :]

def _rope_1d(t, ang):
    nf = ang.shape[-1]
    cos = jnp.cos(ang).astype(t.dtype)
    sin = jnp.sin(ang).astype(t.dtype)
    t1, t2 = t[..., :nf], t[..., nf:]
    return jnp.concatenate([t1 * cos - t2 * sin, t2 * cos + t1 * sin], axis=-1)

def _rope_2d(t, ang_r, ang_c):
    half = HEAD_DIM // 2
    return jnp.concatenate([_rope_1d(t[..., :half], ang_r), _rope_1d(t[..., half:], ang_c)], axis=-1)

def _project(h, w_in):
    z = h @ w_in
    widths = (ATT_Q, ATT_KV, ATT_KV, NA_W, NA_W, NA_W, RET_W, RET_W, RET_W)
    counts = (N_ATT_HEADS, N_ATT_KV, N_ATT_KV, N_NA_HEADS, N_NA_HEADS, N_NA_HEADS,
              N_RET_HEADS, N_RET_HEADS, N_RET_HEADS)
    cuts = [int(v) for v in np.cumsum(widths)]
    parts = jnp.split(z, cuts, axis=-1)
    return tuple(_heads(p, hc) for p, hc in zip(parts[:-1], counts)) + (parts[-1],)

def _gqa(q, k, v, qc, kc, vc, q_g, k_g, ang_r, ang_c, with_ctx_out):
    b, hq, n, d = q.shape
    grp = hq // N_ATT_KV
    scale = d ** -0.5
    q = _rope_2d(_rms(q, q_g), ang_r, ang_c)
    k = _rope_2d(_rms(k, k_g), ang_r, ang_c)
    kc = _rms(kc, k_g)
    k_all = jnp.concatenate([k, kc], axis=2)
    v_all = jnp.concatenate([v, vc], axis=2)
    nblk = n // Q_BLOCK
    qb = q.reshape(b, N_ATT_KV, grp, nblk, Q_BLOCK, d).transpose(3, 0, 1, 2, 4, 5)

    def block(qi):
        s = jnp.einsum('bhgqd,bhkd->bhgqk', qi, k_all).astype(jnp.float32) * scale
        p = jax.nn.softmax(s, axis=-1).astype(v_all.dtype)
        return jnp.einsum('bhgqk,bhkd->bhgqd', p, v_all)

    o = lax.map(block, qb).transpose(1, 2, 3, 0, 4, 5).reshape(b, hq, n, d)
    if not with_ctx_out:
        return o, None
    cl = qc.shape[2]
    qcn = _rms(qc, q_g).reshape(b, N_ATT_KV, grp, cl, d)
    s = jnp.einsum('bhgqd,bhkd->bhgqk', qcn, kc).astype(jnp.float32) * scale
    p = jax.nn.softmax(s, axis=-1).astype(vc.dtype)
    oc = jnp.einsum('bhgqk,bhkd->bhgqd', p, vc).reshape(b, hq, cl, d)
    return o, oc

def _neigh_attn(q, k, v, qc, kc, vc, rpb, with_ctx_out):
    b, h, n, d = q.shape
    rows = n // GRID_W
    wr = min(NA_WIN_ROWS, rows)
    wc = NA_WIN_COLS
    nkeys = wr * GRID_W
    scale = d ** -0.5
    r = jnp.arange(rows)
    ridx = jnp.clip(r - wr // 2, 0, rows - wr)[:, None] + jnp.arange(wr)[None, :]
    col = jnp.arange(GRID_W)
    cstart = jnp.clip(col - wc // 2, 0, GRID_W - wc)
    col_ok = (col[None, :] >= cstart[:, None]) & (col[None, :] < cstart[:, None] + wc)
    mask = jnp.tile(col_ok, (1, wr))
    dr = ridx - r[:, None] + (NA_WIN_ROWS - 1)
    dc = jnp.clip(col[None, :] - col[:, None] + (wc - 1), 0, 2 * wc - 2)
    bias = rpb[:, dr][..., dc].transpose(0, 1, 3, 2, 4).reshape(h, rows, GRID_W, nkeys)

    def grid(t):
        return t.reshape(b, h, rows, GRID_W, d)

    kg = jnp.take(grid(k), ridx, axis=2).reshape(b, h, rows, nkeys, d)
    vg = jnp.take(grid(v), ridx, axis=2).reshape(b, h, rows, nkeys, d)
    qr = grid(q) * scale
    s_nb = jnp.einsum('bhrqd,bhrkd->bhrqk', qr, kg).astype(jnp.float32) + bias.astype(jnp.float32)[None]
    s_nb = jnp.where(mask[None, None, None], s_nb, NEG_INF)
    s_cx = jnp.einsum('bhrqd,bhkd->bhrqk', qr, kc).astype(jnp.float32)
    p = jax.nn.softmax(jnp.concatenate([s_nb, s_cx], axis=-1), axis=-1).astype(v.dtype)
    o = (jnp.einsum('bhrqk,bhrkd->bhrqd', p[..., :nkeys], vg)
         + jnp.einsum('bhrqk,bhkd->bhrqd', p[..., nkeys:], vc)).reshape(b, h, n, d)
    if not with_ctx_out:
        return o, None
    sc = jnp.einsum('bhqd,bhkd->bhqk', qc * scale, kc).astype(jnp.float32)
    pc = jax.nn.softmax(sc, axis=-1).astype(vc.dtype)
    return o, jnp.einsum('bhqk,bhkd->bhqd', pc, vc)

def _ret_chunk_states(k, v, log_g, s0):
    b, h, L, d = k.shape
    nc = L // RET_CHUNK
    kc = k.reshape(b, h, nc, RET_CHUNK, d)
    vc = v.reshape(b, h, nc, RET_CHUNK, d)
    pos = jnp.arange(RET_CHUNK, dtype=jnp.float32)
    zeta = jnp.exp(log_g[:, None] * (RET_CHUNK - 1.0 - pos)[None, :])
    u = jnp.einsum('bhnjd,bhnje->nbhde', kc * zeta[None, :, None, :, None], vc)
    decay = jnp.exp(log_g * RET_CHUNK)[None, :, None, None]

    def step(s, u_n):
        return decay * s + u_n, s

    s_fin, s_before = lax.scan(step, s0, u)
    return s_before, s_fin

def _ret_chunk_out(q, k, v, log_g, s_before):
    b, h, L, d = q.shape
    nc = L // RET_CHUNK
    qc = q.reshape(b, h, nc, RET_CHUNK, d)
    kc = k.reshape(b, h, nc, RET_CHUNK, d)
    vc = v.reshape(b, h, nc, RET_CHUNK, d)
    pos = jnp.arange(RET_CHUNK, dtype=jnp.float32)
    diff = pos[:, None] - pos[None, :]
    dmat = jnp.where(diff >= 0, jnp.exp(log_g[:, None, None] * jnp.maximum(diff, 0.0)[None]), 0.0)
    scores = jnp.einsum('bhnid,bhnjd->bhnij', qc, kc) * dmat[None, :, None]
    inner = jnp.einsum('bhnij,bhnjd->bhnid', scores, vc)
    xi = jnp.exp(log_g[:, None] * (pos + 1.0)[None, :])
    cross = jnp.einsum('bhnid,nbhde->bhnie', qc * xi[None, :, None, :, None], s_before)
    return (inner + cross).reshape(b, h, L, d)

def _retention(q, k, v, qc, kc, vc, log_g2, with_ctx_out):
    dt = q.dtype
    ks = HEAD_DIM ** -0.5
    f32 = lambda t: t.astype(jnp.float32)
    ql, kl, vl = f32(q), f32(k) * ks, f32(v)
    qx, kx, vx = f32(qc), f32(kc) * ks, f32(vc)
    b, h, _, d = ql.shape
    s0 = jnp.zeros((b, h, d, d), jnp.float32)

    def one_direction(ql, kl, vl, qx, kx, vx, lg):
        sb_c, sf_c = _ret_chunk_states(kx, vx, lg, s0)
        ol = _ret_chunk_out(ql, kl, vl, lg, _ret_chunk_states(kl, vl, lg, sf_c)[0])
        oc = _ret_chunk_out(qx, kx, vx, lg, sb_c) if with_ctx_out else None
        return ol, oc

    flip = lambda t: t[:, :, ::-1]
    ol_f, oc_f = one_direction(ql, kl, vl, qx, kx, vx, log_g2[0])
    ol_b, oc_b = one_direction(*map(flip, (ql, kl, vl, qx, kx, vx)), log_g2[1])
    out_lat = (ol_f + flip(ol_b)).astype(dt)
    out_ctx = (oc_f + flip(oc_b)).astype(dt) if with_ctx_out else None
    return out_lat, out_ctx

def _merge(o_a, o_n, o_r, g_r, mix_g, w_out):
    ga, gn, gr = jnp.split(mix_g, [ATT_Q, ATT_Q + NA_W])
    y = jnp.concatenate([_head_norm(_flat(o_a), ga),
                         _head_norm(_flat(o_n), gn),
                         _head_norm(_flat(o_r), gr) * jax.nn.silu(g_r)], axis=-1)
    return y @ w_out

def _moe(h, w_router, b_router, w1, w3, w2):
    per = N_EXPERTS // N_EXPERT_GROUPS
    logits = jnp.einsum('btd,de->bte', h, w_router).astype(jnp.float32) + b_router.astype(jnp.float32)
    probs = jax.nn.softmax(logits, axis=-1)
    pg = probs.reshape(probs.shape[:-1] + (N_EXPERT_GROUPS, per))
    gscore = lax.top_k(pg, TOP_K)[0].sum(-1)
    gsel = jax.nn.one_hot(lax.top_k(gscore, TOP_GROUPS)[1], N_EXPERT_GROUPS, dtype=jnp.float32).sum(-2)
    cand = (pg * gsel[..., None]).reshape(probs.shape)
    w, idx = lax.top_k(cand, TOP_K)
    w = w / w.sum(-1, keepdims=True)
    gates = (jax.nn.one_hot(idx, N_EXPERTS, dtype=jnp.float32) * w[..., None]).sum(-2).astype(h.dtype)
    out = jnp.zeros_like(h)
    for e in range(N_EXPERTS):
        act = jax.nn.silu(h @ w1[e]) * (h @ w3[e])
        out = out + gates[..., e:e + 1] * (act @ w2[e])
    return out

def _layer(x, xc, mod, mod_c, n1_g, n2_g, w_in, q_g, k_g, rpb, log_g2, mix_g, w_out,
           w_router, b_router, w1, w3, w2, ang_r, ang_c, last):
    sh1, sc1, gt1, sh2, sc2, gt2 = jnp.split(mod[:, None, :], 6, axis=-1)
    csh1, csc1, cgt1, csh2, csc2, cgt2 = jnp.split(mod_c, 6, axis=-1)
    want_ctx = not last
    h = _rms(x, n1_g) * (1 + sc1) + sh1
    hc = _rms(xc, n1_g) * (1 + csc1) + csh1
    aq, ak, av, nq, nk, nv, rq, rk, rv, rg = _project(h, w_in)
    caq, cak, cav, cnq, cnk, cnv, crq, crk, crv, crg = _project(hc, w_in)
    o_a, oc_a = _gqa(aq, ak, av, caq, cak, cav, q_g, k_g, ang_r, ang_c, want_ctx)
    o_n, oc_n = _neigh_attn(nq, nk, nv, cnq, cnk, cnv, rpb, want_ctx)
    o_r, oc_r = _retention(rq, rk, rv, crq, crk, crv, log_g2, want_ctx)
    x = x + gt1 * _merge(o_a, o_n, o_r, rg, mix_g, w_out)
    h2 = _rms(x, n2_g) * (1 + sc2) + sh2
    if last:
        return x + gt2 * _moe(h2, w_router, b_router, w1, w3, w2), None
    xc = xc + cgt1 * _merge(oc_a, oc_n, oc_r, crg, mix_g, w_out)
    h2c = _rms(xc, n2_g) * (1 + csc2) + csh2
    n = x.shape[1]
    m = _moe(jnp.concatenate([h2, h2c], axis=1), w_router, b_router, w1, w3, w2)
    return x + gt2 * m[:, :n], xc + cgt2 * m[:, n:]

def setup_inputs(seed: int = 0) -> dict:
    key = jax.random.key(seed)
    ks = jax.random.split(key, 21)
    nrm = jax.random.normal
    f = jnp.float32
    sd = D_MODEL ** -0.5
    decay_init = jnp.log(2.0 ** (5.0 + jnp.arange(N_RET_HEADS, dtype=f)) - 1.0)
    return {
        'x': nrm(ks[0], (BATCH, SEQ, D_MODEL), f),
        'c': nrm(ks[1], (BATCH, D_MODEL), f),
        'ctx': nrm(ks[2], (BATCH, CTX_LEN, D_MODEL), f),
        'c_ctx': nrm(ks[3], (D_MODEL,), f),
        'w_ada': nrm(ks[4], (DEPTH, D_MODEL, 6 * D_MODEL), f) * (0.5 * sd),
        'b_ada': 0.02 * nrm(ks[5], (DEPTH, 6 * D_MODEL), f),
        'norm1_g': 1.0 + 0.02 * nrm(ks[6], (DEPTH, D_MODEL), f),
        'norm2_g': 1.0 + 0.02 * nrm(ks[7], (DEPTH, D_MODEL), f),
        'w_in': nrm(ks[8], (DEPTH, D_MODEL, IN_COLS), f) * sd,
        'q_norm_g': 1.0 + 0.02 * nrm(ks[9], (DEPTH, HEAD_DIM), f),
        'k_norm_g': 1.0 + 0.02 * nrm(ks[10], (DEPTH, HEAD_DIM), f),
        'na_rpb': 0.1 * nrm(ks[11], (DEPTH, N_NA_HEADS, 2 * NA_WIN_ROWS - 1, 2 * NA_WIN_COLS - 1), f),
        'ret_decay': decay_init[None, None, :] + 0.05 * nrm(ks[12], (DEPTH, 2, N_RET_HEADS), f),
        'mix_g': 1.0 + 0.02 * nrm(ks[13], (DEPTH, MIX_W), f),
        'w_out': nrm(ks[14], (DEPTH, MIX_W, D_MODEL), f) * MIX_W ** -0.5,
        'w_router': nrm(ks[15], (D_MODEL, N_EXPERTS), f) * sd,
        'b_router': 0.01 * nrm(ks[16], (N_EXPERTS,), f),
        'w_exp1': nrm(ks[17], (DEPTH, N_EXPERTS, D_MODEL, D_EXPERT), f) * sd,
        'w_exp3': nrm(ks[18], (DEPTH, N_EXPERTS, D_MODEL, D_EXPERT), f) * sd,
        'w_exp2': nrm(ks[19], (DEPTH, N_EXPERTS, D_EXPERT, D_MODEL), f) * D_EXPERT ** -0.5,
        'final_g': 1.0 + 0.02 * nrm(ks[20], (D_MODEL,), f),
    }

def reference(x, c, ctx, c_ctx, w_ada, b_ada, norm1_g, norm2_g, w_in, q_norm_g, k_norm_g,
              na_rpb, ret_decay, mix_g, w_out, w_router, b_router, w_exp1, w_exp3, w_exp2, final_g):
    ang_r, ang_c = _axial_angles(x.shape[1])
    sc = jax.nn.silu(c)
    scc = jax.nn.silu(c_ctx)
    xc = ctx
    for l in range(DEPTH):
        mod = sc @ w_ada[l] + b_ada[l]
        mod_c = scc @ w_ada[l] + b_ada[l]
        log_g2 = jax.nn.log_sigmoid(ret_decay[l].astype(jnp.float32))
        x, xc = _layer(x, xc, mod, mod_c, norm1_g[l], norm2_g[l], w_in[l], q_norm_g[l], k_norm_g[l],
                       na_rpb[l], log_g2, mix_g[l], w_out[l], w_router, b_router,
                       w_exp1[l], w_exp3[l], w_exp2[l], ang_r, ang_c, l == DEPTH - 1)
    return _rms(x, final_g)


_drawn_inputs = setup_inputs


def setup_inputs(seed=0):
    import zlib

    import numpy as np

    out = dict(_drawn_inputs(seed))
    spreads = {}
    factors = {'q_norm_g': 8.0, 'k_norm_g': 8.0, 'na_rpb': 2.988, 'mix_g': 2.745, 'final_g': 2.939}
    for name, (base, spread) in spreads.items():
        noise = np.random.default_rng([zlib.crc32(name.encode()), seed]).standard_normal(out[name].shape)
        drawn = base * np.exp(spread * noise) if base else spread * noise
        out[name] = __import__('jax').numpy.asarray(drawn.astype(out[name].dtype))
    for name, factor in factors.items():
        out[name] = (out[name] * factor).astype(out[name].dtype)
    return out
```

```python
from contextlib import ExitStack

import numpy as np

import concourse.bass as bass
from concourse import mybir

F32 = mybir.dt.float32
I32 = mybir.dt.int32
U32 = mybir.dt.uint32
ALU = mybir.AluOpType
ACT = mybir.ActivationFunctionType
X_AXIS = mybir.AxisListType.X

P = 128
D = 1024
DEPTH = 2
KD = D // P
SEQ = 256
CTX = 256
NT = (SEQ + CTX) // P
LT = SEQ // P
HD = 64
GRID_W = 64
IN_COLS = 2944
N_EXP = 16
F = 512
KF = F // P
EPS = 1e-6
NEG = -1e30
HALF = 512
HPR = 15 * 31
TOP = 8

A_Q, A_K, A_V = 0, 384, 512
N_Q, N_K, N_V = 640, 896, 1152
R_Q, R_K, R_V, R_G = 1408, 1792, 2176, 2560

OV_MAX = [7, 3]
SLOT_T = [N_EXP + n for n in OV_MAX]

RING = 6
N_ADA, N_WIN, N_WOUT, N_MOE = 12, 6, 2, 3 * N_EXP
ADA_START = range(0, 4)
ADA_NORM = range(4, 6)
ADA_RET = range(6, 12)
ADA_ROUTE = range(12, 16)
ADA_SLOTS = range(16, 19)
ADA_COMBINE = range(19, 22)
ADA_LAST = range(22, 24)
_ada_first = [0] * (DEPTH * N_ADA)
WIN0, WOUT0, MOE0 = [0] * DEPTH, [0] * DEPTH, [0] * DEPTH
STREAM = [("ada", ADA_START), ("ada", ADA_NORM), ("win", 0), ("ada", ADA_RET), ("wout", 0), ("ada", ADA_ROUTE),
          ("ada", ADA_SLOTS), ("moe", 0), ("ada", ADA_COMBINE), ("win", 1), ("wout", 1), ("ada", ADA_LAST),
          ("moe", 1)]
_b = 0
for _kind, _what in STREAM:
    if _kind == "ada":
        for _job in _what:
            _ada_first[_job] = _b
            _b += 1
    else:
        {"win": WIN0, "wout": WOUT0, "moe": MOE0}[_kind][_what] = _b
        _b += {"win": N_WIN, "wout": N_WOUT, "moe": N_MOE}[_kind]
ADA_BLOCK = tuple(_ada_first)
ADA_RUNS = ((0, 6), (6, 12), (12, 22), (22, 24))


def q_tiles(l):
    return NT if l < DEPTH - 1 else LT


def win_cols(n):
    return min(HALF, IN_COLS - n * HALF)


def needed(l, t, n):
    width = win_cols(n)
    if t < q_tiles(l):
        return [(0, width)]
    out = []
    for a, b in ((A_K, N_Q), (N_K, R_Q), (R_K, R_G)):
        a, b = max(a - n * HALF, 0), min(b - n * HALF, width)
        if a < b:
            out.append((a, b))
    return out


PROJ = [[(n, t) for n in range(N_WIN) for t in range(NT) if needed(l, t, n)] for l in range(DEPTH)]
PROJ_BEFORE = [0, len(PROJ[0])]
PROJ_BANKS = [6, 7, 0, 1]

ROWS_BEFORE = {}
_n = 0
for _l in range(DEPTH):
    for _what, _count in (("norm1", NT), ("merge", q_tiles(_l)), ("norm2", q_tiles(_l))):
        ROWS_BEFORE[_l, _what] = _n
        _n += _count

PAIRS = {
    "A": [(A_Q + 128 * i, True) for i in range(3)] + [(A_K, False)],
    "N": [(N_Q, True), (N_Q + 128, True), (N_K, False), (N_K + 128, False)],
    "R": [(R_Q + 128 * i, True) for i in range(3)] + [(R_K + 128 * i, False) for i in range(3)],
}
PAIR_SLOT = {"A": 0, "N": 4, "R": 0}
PAIR_FIRST = {"A": 0, "N": 4, "R": 8}
N_PAIRS = 14


def units(l):
    out = []
    for h in range(6):
        for t in range(q_tiles(l)):
            out.append(dict(q=h % 3, base=64 * (h // 3), k=3, v=A_V + 64 * (h // 3), o=A_Q + 64 * h, t=t, bias=None))
    for h in range(4):
        for t in range(q_tiles(l)):
            out.append(dict(q=4 + h // 2, base=64 * (h % 2), k=6 + h // 2, v=N_V + 64 * h, o=N_Q + 64 * h, t=t,
                            bias=h if t < LT else None))
    for u in out:
        u["keys"] = list(range(NT)) if u["t"] < LT else list(range(LT, NT))
    return out


UNITS = [units(l) for l in range(DEPTH)]
UNITS_BEFORE = [0, len(UNITS[0])]
N_RH = 6
MERGED = ((A_Q, 0, 384), (N_Q, 384, 256), (R_Q, 640, 384))


def ret_jobs(l):
    jobs = [((0, 1), 0, "near"), ((2, 3), 0, "far")]
    return jobs + ([((2, 3), 256, "near")] if l < DEPTH - 1 else [])


RJ_BEFORE = [0, N_RH * len(ret_jobs(0))]
RET_BANK = [0, 1, 6]
SCORE_BANK = [0, 1, 6]
LAGS = 384

CONST = {}
_c = 0
for _name, _w in (("ident", 128), ("tri", 128), ("ones", 128), ("lag", 384), ("ahead", 384), ("cos", 128), ("sin", 128),
                  ("mask", 64), ("down", 16), ("up", 16)):
    CONST[_name] = (_c, _w)
    _c += _w
N_CONST = _c


def constants():
    c = np.zeros((P, N_CONST), np.float32)

    def put(name, v):
        a, w = CONST[name]
        c[:, a:a + w] = np.asarray(v, np.float32).reshape(P, w)

    p = np.arange(P)
    put("ident", np.eye(P))
    put("tri", p[:, None] < p[None, :])
    put("ones", np.ones((P, P)))
    lag = np.arange(384)[None, :] - 128 - p[:, None]
    put("lag", lag)
    put("ahead", np.maximum(lag, 0))
    inv = np.float32(10000.0) ** (-np.arange(16, dtype=np.float32) / np.float32(16))
    cos, sin = np.zeros((P, 2, 64)), np.zeros((P, 2, 64))
    for t in range(2):
        tok = t * P + p
        for half, pos in enumerate((tok // GRID_W, tok % GRID_W)):
            ang = (pos.astype(np.float32)[:, None] * inv[None, :]).astype(np.float32).astype(np.float64)
            o = 32 * half
            cos[:, t, o:o + 16] = cos[:, t, o + 16:o + 32] = np.cos(ang)
            sin[:, t, o:o + 16] = -np.sin(ang)
            sin[:, t, o + 16:o + 32] = np.sin(ang)
    put("cos", cos)
    put("sin", sin)
    col = np.arange(GRID_W)
    start = np.clip(col - 8, 0, GRID_W - 16)
    ok = (col[None, :] >= start[:, None]) & (col[None, :] < start[:, None] + 16)
    put("mask", np.where(ok, 0.0, NEG)[p % GRID_W])
    put("down", np.tile(16 - np.arange(16), (P, 1)))
    put("up", np.tile(np.arange(16), (P, 1)))
    ids = np.zeros((P, SLOT_T[0] + NT), np.uint32)
    ids[:, SLOT_T[0]:] = np.arange(NT)[None, :] * P + p[:, None]
    return c, ids, np.zeros((P, D), np.float32)


def trunk(nc, g, out):
    mod_d = nc.dram_tensor("mod_scratch", [DEPTH, 2, 6 * D], F32).ap()
    rpb_d = nc.dram_tensor("rpb_scratch", [DEPTH * 4 * 15, 128], F32).ap()
    near_d = nc.dram_tensor("bias_scratch", [DEPTH * 4 * 15, GRID_W, GRID_W], F32).ap()
    h2_d = [nc.dram_tensor(f"h2_scratch{l}", [q_tiles(l) * P, D], F32).ap() for l in range(DEPTH)]
    slot_d = [nc.dram_tensor(f"slot_token_scratch{l}", [P * SLOT_T[l], 1], U32).ap() for l in range(DEPTH)]
    y_d = [nc.dram_tensor(f"y_scratch{l}", [P * SLOT_T[l], D], F32).ap() for l in range(DEPTH)]

    with ExitStack() as ctx:
        def sb(name, shape, dt=F32):
            return ctx.enter_context(nc.sbuf_tensor("sb_" + name, shape, dt))

        def sem(name):
            return ctx.enter_context(nc.semaphore(name))

        X = sb("x", [P, NT, D])
        T = sb("transposed", [P, 8, NT * P])
        Z = sb("z", [P, NT * IN_COLS])
        ring = sb("ring", [P, RING, 4096])
        R1 = sb("r1", [P, 2, 1024])
        R2 = sb("r2", [P, 2, 1024])
        R3 = sb("r3", [P, 2, 1024])
        C = sb("constants", [P, N_CONST])
        ids = sb("ids", [P, SLOT_T[0] + NT], U32)
        c_raw = sb("c_raw", [P, 2, KD])
        c_col = sb("c_col", [P, KD, 2])
        w_rt = sb("w_router", [P, KD, N_EXP])
        b_rt = sb("b_router", [P, N_EXP])
        qk_gain = sb("qk_gain", [P, DEPTH, 2, HD])
        lg = sb("log_decay", [P, 4, 2 * DEPTH * N_RH])
        lgt = sb("log_decay_tmp", [P, 2, 2 * DEPTH * N_RH])
        eps = sb("eps", [P, 1])
        ss = sb("row_ss", [P, 24])
        rstd = sb("row_rstd", [P, 24])
        hss = sb("head_ss", [P, NT, 16])
        hr = sb("head_rstd", [P, NT, 16])
        soft = sb("soft", [P, 3, 4])
        rw = sb("route_w", [P, NT, 2])
        slots = sb("route_slots", [P, NT, 2], U32)
        ovinfo = sb("overflow_info", [1, TOP], I32)
        slot_tok = sb("slot_tokens", [P, SLOT_T[0]], U32)

        z = Z[:].rearrange("p (t c) -> p t c", t=NT)
        rowbuf = R2
        tables_flat = R1[:].rearrange("p a b -> p (a b)")
        near_tab = [tables_flat[:, 2 * LAGS * i:2 * LAGS * i + LAGS] for i in range(2)]
        far_tab = [tables_flat[:, 2 * LAGS * i + LAGS:2 * LAGS * (i + 1)] for i in range(2)]
        behind = tables_flat[:, 4 * LAGS:5 * LAGS]
        ident = C[:, CONST["ident"][0]:CONST["ident"][0] + 128]

        def const(name):
            a, w = CONST[name]
            return C[:, a:a + w]

        ps = ctx.enter_context(nc.psum_tensor("ps", [P, 8, HALF], F32))

        w_full = [sem(f"w_full{i}") for i in range(RING)]
        w_used = sem("w_used")
        in_c, in_x, in_tables, in_const, in_decay = sem("in_c"), sem("in_x"), sem("in_tables"), sem("in_const"), sem("in_decay")
        in_rpb, rpb_out, bias_spread = sem("in_rpb"), sem("rpb_out"), sem("bias_spread")
        in_brow = [sem(f"in_brow{i}") for i in range(2)]
        mod_out = [sem(f"mod_out{i}") for i in range(2)]
        in_rows, in_mix, in_gate, in_bias = sem("in_rows"), sem("in_mix"), sem("in_gate"), sem("in_bias")
        h2_out = [sem(f"h2_out{i}") for i in range(2)]
        y_zero, slot_zero, slot_out, slot_in = sem("y_zero"), sem("slot_zero"), sem("slot_out"), sem("slot_in")
        xg_in = [sem(f"xg_in{i}") for i in range(2)]
        y_out = [sem(f"y_out{i}") for i in range(2)]
        yg_in = [sem(f"yg_in{i}") for i in range(2)]
        ov_w_in = [sem(f"ov_w_in{l}") for l in range(DEPTH)]
        ov_xg_in = [sem(f"ov_xg_in{l}") for l in range(DEPTH)]
        ov_y_out = [sem(f"ov_y_out{l}") for l in range(DEPTH)]
        fin_in, res_out = sem("fin_in"), sem("res_out")
        dve_step, act_step = sem("dve_step"), sem("act_step")
        pad_zero, eps_set = sem("pad_zero"), sem("eps_set")
        silu_c, decay_u, decay_ready = sem("silu_c"), sem("decay_u"), sem("decay_ready")
        ada_mm, ada_ev = sem("ada_mm"), sem("ada_ev")
        row_sq, row_std, row_ready = sem("row_sq"), sem("row_std"), sem("row_ready")
        rowT_mm, rowT_act, rowT_dve = sem("rowT_mm"), sem("rowT_act"), sem("rowT_dve")
        proj_mm, proj_act, proj_dve = sem("proj_mm"), sem("proj_act"), sem("proj_dve")
        qk_ss, qk_std, qk_ready = sem("qk_ss"), sem("qk_std"), sem("qk_ready")
        bias_ready, na_done = sem("bias_ready"), sem("na_done")
        pair_mm, pair_act, pair_dve = sem("pair_mm"), sem("pair_act"), sem("pair_dve")
        score_mm, max_ready, probs_ready = sem("score_mm"), sem("max_ready"), sem("probs_ready")
        pT_mm, pT_ev, o_mm, o_ev = sem("pT_mm"), sem("pT_ev"), sem("o_mm"), sem("o_ev")
        behind_ready, decay_exp, w_ready = sem("behind_ready"), sem("decay_exp"), sem("w_ready")
        rscore_mm, rscore_w, ro_mm, ro_ev = sem("rscore_mm"), sem("rscore_w"), sem("ro_mm"), sem("ro_ev")
        mg_sq, mg_ss, mg_std, silu_g = sem("mg_sq"), sem("mg_ss"), sem("mg_std"), sem("silu_g")
        wout_mm, x_upd = sem("wout_mm"), sem("x_upd")
        rt_mm, rt_max, rt_exp, rt_sel, rank_mm = sem("rt_mm"), sem("rt_max"), sem("rt_exp"), sem("rt_sel"), sem("rank_mm")
        slots_ready = sem("slots_ready")
        xT_mm, xT_act, xT_dve = sem("xT_mm"), sem("xT_act"), sem("xT_dve")
        silu_h, act_ready = sem("silu_h"), sem("act_ready")
        aT_mm, aT_ev, y_mm, y_act, y_dve = sem("aT_mm"), sem("aT_ev"), sem("y_mm"), sem("y_act"), sem("y_dve")
        ov_pe = [sem(f"ov_pe{l}") for l in range(DEPTH)]
        ov_act = [sem(f"ov_act{l}") for l in range(DEPTH)]
        ov_dve = [sem(f"ov_dve{l}") for l in range(DEPTH)]
        comb_mul, moe_x, fin_ready = sem("comb_mul"), sem("moe_x"), sem("fin_ready")

        def full(b):
            return w_full[b % RING], 16 * (b // RING + 1)

        def modrow(job):
            return R3[0:2, 1, (job % 2) * HALF:(job % 2 + 1) * HALF]

        def moe_block(l, e, m):
            if m == 2:
                return MOE0[l] + 3 * e + (3 if e < N_EXP - 1 else 2)
            return MOE0[l] + (m if e == 0 else 3 * e - 1 + 2 * m)

        xg = [Z[:, 1024 * i:1024 * (i + 1)] for i in range(2)]
        xgT = [Z[:, 2048 + 1024 * i:3072 + 1024 * i].rearrange("p (k t) -> p k t", k=KD) for i in range(2)]
        s1 = Z[:, 4096:4608]
        act_sb = Z[:, 4608:5120]
        actT = [Z[:, 5120 + HALF * i:5632 + HALF * i].rearrange("p (k t) -> p k t", k=KF) for i in range(2)]
        ybuf = [Z[:, 6144 + 1024 * i:7168 + 1024 * i] for i in range(2)]
        yg = [Z[:, 5120 + 2048 * i:5120 + 2048 * (i + 1)].rearrange("p (k c) -> p k c", k=2) for i in range(2)]
        rtmp = Z[:, 8192:8192 + 30 * 64 + 64]
        rows = [Z[:, 1024 * i:1024 * (i + 1)] for i in range(5)]

        def overflow(eng, l, tile, ready):
            eng.wait_ge(slots_ready, l + 1)
            n_ov = eng.value_load(ovinfo[0:1, 0:1], min_val=0, max_val=OV_MAX[0])
            with eng.If(n_ov > 0):
                ready()
                tile(0, n_ov)
                for t in range(1, OV_MAX[l]):
                    with eng.If(n_ov > t):
                        tile(t, n_ov)
                    eng.nop()
            eng.nop()

        block = ctx.enter_context(nc.Block())

        @block.sync
        def _(sp):
            def load(b, dst, src):
                if b >= RING:
                    sp.wait_ge(w_used, b - RING + 1)
                sp.dma_start(dst, src).then_inc(full(b)[0], 16)

            def slot(b):
                return ring[:, b % RING, :]

            def ada(jobs):
                for job in jobs:
                    b, l, n = ADA_BLOCK[job], job // N_ADA, job % N_ADA
                    load(b, slot(b).rearrange("p (k c) -> p k c", k=KD),
                         g["w_ada"][l].rearrange("(p k) c -> p k c", k=KD)[:, :, n * HALF:(n + 1) * HALF])

            def w13(w, l, e):
                return w[l, e].rearrange("(p k) f -> p (k f)", k=KD)

            def w2(l, e):
                return g["w_exp2"][l, e].rearrange("(p k) c -> p (k c)", k=KF)

            sp.dma_start(c_raw[:, 0, :], g["c"].rearrange("o (p k) -> p (o k)", k=KD)).then_inc(in_c, 16)
            sp.dma_start(c_raw[:, 1, :], g["c_ctx"].rearrange("(p k) -> p k", k=KD)).then_inc(in_c, 16)
            ada(ADA_START)
            ada(ADA_NORM)
            for l in range(DEPTH):
                for n in range(N_WIN):
                    if n == l:
                        sp.wait_ge(in_rows, 16 * ROW_LOADS[2 * l])
                    b, c = WIN0[l] + n, win_cols(n)
                    load(b, slot(b)[:, 0:KD * c].rearrange("p (k c) -> p k c", k=KD),
                         g["w_in"][l].rearrange("(p k) c -> p k c", k=KD)[:, :, n * HALF:n * HALF + c])
                if l == 0:
                    ada(ADA_RET)
                for n in range(N_WOUT):
                    b = WOUT0[l] + n
                    load(b, slot(b).rearrange("p (k c) -> p k c", k=KD),
                         g["w_out"][l].rearrange("(p k) c -> p k c", k=KD)[:, :, n * HALF:(n + 1) * HALF])
                if l == 0:
                    ada(ADA_ROUTE)
                    ada(ADA_SLOTS)
                else:
                    ada(ADA_LAST)
                load(moe_block(l, 0, 0), slot(moe_block(l, 0, 0)), w13(g["w_exp1"], l, 0))
                load(moe_block(l, 0, 1), slot(moe_block(l, 0, 1)), w13(g["w_exp3"], l, 0))

                def turn(e, b0, off):
                    for m, src in enumerate((w13(g["w_exp1"], l, e), w2(l, e - 1), w13(g["w_exp3"], l, e))):
                        b = b0 + m
                        sp.wait_ge(w_used, off + b - RING + 1)
                        sp.dma_start(slot(b), src).then_inc(full(b)[0], 16)

                turn(1, moe_block(l, 1, 0), 0)
                turn(2, moe_block(l, 2, 0), 0)
                with sp.Fori(0, (N_EXP - 4) // 2) as i:
                    for e in (3, 4):
                        turn(i * 2 + e, moe_block(l, e, 0), i * RING)
                turn(N_EXP - 1, moe_block(l, N_EXP - 1, 0), 0)
                b = moe_block(l, N_EXP - 1, 2)
                load(b, slot(b), w2(l, N_EXP - 1))

                def ov_tile(t, n_ov):
                    eid = sp.value_load(ovinfo[0:1, 1 + t:2 + t], min_val=0, max_val=N_EXP - 1)
                    for m, src in enumerate((w13(g["w_exp1"], l, eid), w13(g["w_exp3"], l, eid), w2(l, eid))):
                        sp.dma_start(ring[:, m, :], src).then_inc(ov_w_in[l], 16)
                    sp.wait_ge(ov_pe[l], 4 * t + 4)
                    sp.nop()

                overflow(sp, l, ov_tile, lambda: sp.wait_ge(w_used, MOE0[l] + N_MOE))
                if l == 0:
                    ada(ADA_COMBINE)

        @block.tensor
        def _(pe):
            mm, tp = nc.tensor.matmul, nc.tensor.transpose

            def ada(jobs, bank0=0):
                for job in jobs:
                    b = ADA_BLOCK[job]
                    if job >= 2:
                        pe.wait_ge(ada_ev, job - 1)
                    pe.wait_ge(*full(b))
                    w = ring[:, b % RING, :].rearrange("p (k c) -> p k c", k=KD)
                    for k in range(KD):
                        last = mm(ps[0:2, bank0 + job % 2, :], c_col[:, k, :], w[:, k, :], start=(k == 0), stop=(k == KD - 1))
                    last.then_inc(w_used, 1)

            def rows_transposed(n):
                pe.wait_ge(row_ready, n + 1)
                if n >= 2:
                    pe.wait_ge(rowT_act, n - 1)
                    pe.wait_ge(rowT_dve, n - 1)
                src = rowbuf[:, n % 2, :].rearrange("p (c k) -> p k c", k=KD)
                for half in range(2):
                    for q in range(4):
                        last = tp(ps[:, 2 + 2 * (n % 2) + half, q * P:(q + 1) * P], src[:, 4 * half + q, :], ident)
                    last.then_inc(rowT_mm, 1)

            def projection(l):
                first = ROWS_BEFORE[l, "norm1"]
                rows_transposed(first)
                rows_transposed(first + 1)
                pe.wait_ge(ada_ev, (ADA_COMBINE if l else ADA_NORM)[-1] + 1)
                for i, (n, t) in enumerate(PROJ[l]):
                    job, b = PROJ_BEFORE[l] + i, WIN0[l] + n
                    if i < NT:
                        pe.wait_ge(rowT_act, first + t + 1)
                        pe.wait_ge(rowT_dve, first + t + 1)
                    if job >= 4:
                        pe.wait_ge(proj_act if job % 2 == 0 else proj_dve, (job - 4) // 2 + 1)
                    pe.wait_ge(*full(b))
                    w = ring[:, b % RING, 0:KD * win_cols(n)].rearrange("p (k c) -> p k c", k=KD)
                    bank = ps[:, PROJ_BANKS[job % 4], :]
                    for lo, hi in needed(l, t, n):
                        for k in range(KD):
                            last = mm(bank[:, lo:hi], T[:, k, t * P:(t + 1) * P], w[:, k, lo:hi],
                                      start=(k == 0), stop=(k == KD - 1))
                    last.then_inc(proj_mm, 1)
                    if i < NT - 2:
                        rows_transposed(first + i + 2)
                    if i + 1 == len(PROJ[l]) or PROJ[l][i + 1][0] != n:
                        pe.wait_ge(proj_mm, job + 1)
                        pe.sem_inc(w_used, 1)

            def pairs(l, group):
                for i, (c0, is_q) in enumerate(PAIRS[group]):
                    job = l * N_PAIRS + PAIR_FIRST[group] + i
                    if job >= 4:
                        pe.wait_ge(pair_act if job % 2 == 0 else pair_dve, (job - 4) // 2 + 1)
                    for t in range(q_tiles(l) if is_q else NT):
                        last = tp(ps[:, 2 + job % 4, t * P:(t + 1) * P], z[:, t, c0:c0 + P], ident)
                    last.then_inc(pair_mm, 1)

            def pairs_moved(l, group):
                n = (l * N_PAIRS + PAIR_FIRST[group] + len(PAIRS[group])) // 2
                pe.wait_ge(pair_act, n)
                pe.wait_ge(pair_dve, n)

            def attention(l):
                us, before = UNITS[l], UNITS_BEFORE[l]

                def scores(i):
                    u, n = us[i], before + i
                    if n >= 3:
                        pe.wait_ge(probs_ready, n - 2)
                    bank = ps[:, SCORE_BANK[n % 3], :]
                    q = T[u["base"]:u["base"] + HD, u["q"], u["t"] * P:(u["t"] + 1) * P]
                    k = T[u["base"]:u["base"] + HD, u["k"], :]
                    if u["bias"] is None:
                        last = mm(bank[:, 0:P * len(u["keys"])], q, k[:, P * u["keys"][0]:], start=True, stop=True)
                    else:
                        pe.wait_ge(bias_ready, l + 1)
                        bias = R3[:].rearrange("p a b -> p (a b)").rearrange("p (h t k) -> p h t k", h=4, t=2)
                        mm(bank[:, 0:SEQ], q, k[:, 0:SEQ], start=True, stop=False)
                        mm(bank[:, 0:SEQ], ident, bias[:, u["bias"], u["t"], :], start=False, stop=True)
                        last = mm(bank[:, SEQ:], q, k[:, SEQ:], start=True, stop=True)
                    last.then_inc(score_mm, 1)

                def probs_transposed(i):
                    u, n = us[i], before + i
                    pe.wait_ge(probs_ready, n + 1)
                    if n >= 2:
                        pe.wait_ge(pT_ev, n - 1)
                    for c in range(len(u["keys"])):
                        last = tp(ps[:, 2 + n % 2, c * P:(c + 1) * P],
                                  R2[:, 0, (n % 2) * HALF + c * P:(n % 2) * HALF + (c + 1) * P], ident)
                    last.then_inc(pT_mm, 1)

                def output(i):
                    u, n = us[i], before + i
                    pe.wait_ge(pT_ev, n + 1)
                    if n >= 2:
                        pe.wait_ge(o_ev, n - 1)
                    for c, kt in enumerate(u["keys"]):
                        last = mm(ps[:, 4 + n % 2, 0:HD], R2[:, 1, (n % 2) * HALF + c * P:(n % 2) * HALF + (c + 1) * P],
                                  z[:, kt, u["v"]:u["v"] + HD], start=(c == 0), stop=(c == len(u["keys"]) - 1))
                    last.then_inc(o_mm, 1)

                scores(0)
                scores(1)
                for i in range(len(us) + 1):
                    if i + 2 < len(us):
                        scores(i + 2)
                    if i < len(us):
                        probs_transposed(i)
                    if i >= 1:
                        output(i - 1)

            def retention(l):
                jobs, nj = ret_jobs(l), len(ret_jobs(l))

                def scores(r):
                    base, pair = HD * (r % 2), r // 2
                    for j, (keys, q0, _) in enumerate(jobs):
                        job = RJ_BEFORE[l] + r * nj + j
                        if r:
                            pe.wait_ge(rscore_w, job - nj + 1)
                        for kk, kt in enumerate(keys):
                            last = mm(ps[:, RET_BANK[j], (1 - kk) * 256:(2 - kk) * 256],
                                      T[base:base + HD, 3 + pair, kt * P:(kt + 1) * P],
                                      T[base:base + HD, pair, q0:q0 + 256], start=True, stop=True)
                        last.then_inc(rscore_mm, 1)

                def output(r):
                    head = l * N_RH + r
                    pe.wait_ge(rscore_w, RJ_BEFORE[l] + (r + 1) * nj)
                    if head >= 2:
                        pe.wait_ge(ro_ev, head - 1)
                    for t in range(q_tiles(l)):
                        use = (0, 1) if t < LT else (2,)
                        parts = [(j, kk, kt) for j in use for kk, kt in enumerate(jobs[j][0])]
                        for x, (j, kk, kt) in enumerate(parts):
                            job = RJ_BEFORE[l] + r * nj + j
                            at = (1 - kk) * 256 + (t % LT) * P
                            w = R2[:, (job % 4) // 2, (job % 2) * HALF + at:(job % 2) * HALF + at + P]
                            last = mm(ps[:, 7 - 2 * (head % 2), t * HD:(t + 1) * HD], w,
                                      z[:, kt, R_V + HD * r:R_V + HD * (r + 1)],
                                      start=(x == 0), stop=(x == len(parts) - 1))
                    last.then_inc(ro_mm, 1)

                scores(0)
                for r in range(N_RH):
                    if l == 0:
                        ada([ADA_RET[r]], 2)
                    if r + 1 < N_RH:
                        scores(r + 1)
                    output(r)

            def out_projection(l, t):
                n = ROWS_BEFORE[l, "merge"] + t
                pe.wait_ge(rowT_act, n + 1)
                pe.wait_ge(rowT_dve, n + 1)
                for half in range(2):
                    job, b = 2 * (NT * l + t) + half, WOUT0[l] + half
                    if job >= 2:
                        pe.wait_ge(x_upd, job - 1)
                    pe.wait_ge(*full(b))
                    w = ring[:, b % RING, :].rearrange("p (k c) -> p k c", k=KD)
                    for k in range(KD):
                        last = mm(ps[:, 6 + half, :], T[:, k, t * P:(t + 1) * P], w[:, k, :],
                                  start=(k == 0), stop=(k == KD - 1))
                    last.then_inc(wout_mm, 1)

            def router(l):
                n = ROWS_BEFORE[l, "norm2"] + q_tiles(l)
                pe.wait_ge(rowT_act, n)
                pe.wait_ge(rowT_dve, n)
                pe.wait_ge(x_upd, 2 * (NT * l + q_tiles(l)))
                for t in range(q_tiles(l)):
                    for k in range(KD):
                        last = mm(ps[:, 6, t * N_EXP:(t + 1) * N_EXP], T[:, k, t * P:(t + 1) * P], w_rt[:, k, :],
                                  start=(k == 0), stop=(k == KD - 1))
                last.then_inc(rt_mm, 1)

            def ranks(l):
                nq = q_tiles(l)
                pe.wait_ge(rt_sel, l + 1)
                sel = rtmp[:, 0:nq * N_EXP]
                for t in range(nq + 1):
                    for s in range(min(t + 1, nq)):
                        last = mm(ps[:, 7, t * N_EXP:(t + 1) * N_EXP], const("tri" if s == t else "ones"),
                                  sel[:, s * N_EXP:(s + 1) * N_EXP], start=(s == 0), stop=(s == min(t, nq - 1)))
                last.then_inc(rank_mm, 1)

            def x_transposed(src):
                v = src.rearrange("p (c k) -> p k c", k=KD)
                for half in range(2):
                    for q in range(4):
                        last = tp(ps[:, 4 + half, q * P:(q + 1) * P], v[:, 4 * half + q, :], ident)
                    last.then_inc(xT_mm, 1)

            def moe(l):
                def xT(e, i):
                    n = l * N_EXP + e
                    pe.wait_ge(xg_in[e % 2], i * 16 + 16 * (n // 2 + 1))
                    if n:
                        pe.wait_ge(xT_act, i * 2 + n)
                        pe.wait_ge(xT_dve, i * 2 + n)
                    x_transposed(xg[e % 2])

                def h(e, i, m):
                    n, b = l * N_EXP + e, moe_block(l, e, m)
                    if m == 0:
                        pe.wait_ge(xT_act, i * 2 + (n + 1))
                        pe.wait_ge(xT_dve, i * 2 + (n + 1))
                    if n:
                        pe.wait_ge(silu_h if m == 0 else act_ready, i * 2 + n)
                    pe.wait_ge(full(b)[0], i * 16 + full(b)[1])
                    for k in range(KD):
                        last = mm(ps[:, m, :], xgT[e % 2][:, k, :], ring[:, b % RING, k * F:(k + 1) * F],
                                  start=(k == 0), stop=(k == KD - 1))
                    last.then_inc(w_used, 1)

                def aT(e, i):
                    n = l * N_EXP + e
                    pe.wait_ge(act_ready, i * 2 + (n + 1))
                    if n:
                        pe.wait_ge(aT_ev, i * 2 + n)
                    v = act_sb.rearrange("p (c k) -> p k c", k=KF)
                    for k in range(KF):
                        last = tp(ps[:, 6, k * P:(k + 1) * P], v[:, k, :], ident)
                    last.then_inc(aT_mm, 1)

                def y(e, i):
                    n, b = l * N_EXP + e, moe_block(l, e, 2)
                    pe.wait_ge(aT_ev, i * 2 + (n + 1))
                    if n:
                        pe.wait_ge(y_act, i * 2 + n)
                        pe.wait_ge(y_dve, i * 2 + n)
                    pe.wait_ge(full(b)[0], i * 16 + full(b)[1])
                    for half in range(2):
                        for k in range(KF):
                            last = mm(ps[:, 2 + half, :], actT[e % 2][:, k, :],
                                      ring[:, b % RING, k * D + half * HALF:k * D + (half + 1) * HALF],
                                      start=(k == 0), stop=(k == KF - 1))
                        last.then_inc(y_mm if half == 0 else w_used, 1)

                def turn(e, i, more=True):
                    h(e, i, 0)
                    y(e - 1, i)
                    h(e, i, 1)
                    if more:
                        xT(e + 1, i)
                    aT(e, i)

                xT(0, 0)
                h(0, 0, 0)
                h(0, 0, 1)
                xT(1, 0)
                aT(0, 0)
                turn(1, 0)
                turn(2, 0)
                with pe.Fori(0, (N_EXP - 4) // 2) as i:
                    turn(3, i)
                    turn(4, i)
                turn(N_EXP - 1, 0, more=False)
                y(N_EXP - 1, 0)

            def ov_tile(l):
                def tile(t, _):
                    pe.wait_ge(ov_xg_in[l], 16 * (t + 1))
                    v = xg[0].rearrange("p (c k) -> p k c", k=KD)
                    for k in range(KD):
                        last = tp(ps[:, 4 + k // 4, (k % 4) * P:(k % 4 + 1) * P], v[:, k, :], ident)
                    last.then_inc(ov_pe[l], 1)
                    pe.wait_ge(ov_act[l], 4 * t + 1)
                    pe.wait_ge(ov_w_in[l], 48 * (t + 1))
                    for m in range(2):
                        for k in range(KD):
                            last = mm(ps[:, m, :], xgT[0][:, k, :], ring[:, m, k * F:(k + 1) * F],
                                      start=(k == 0), stop=(k == KD - 1))
                    last.then_inc(ov_pe[l], 1)
                    pe.wait_ge(ov_dve[l], t + 1)
                    v = act_sb.rearrange("p (c k) -> p k c", k=KF)
                    for k in range(KF):
                        last = tp(ps[:, 6, k * P:(k + 1) * P], v[:, k, :], ident)
                    last.then_inc(ov_pe[l], 1)
                    pe.wait_ge(ov_act[l], 4 * t + 3)
                    for half in range(2):
                        for k in range(KF):
                            last = mm(ps[:, 2 + half, :], actT[0][:, k, :],
                                      ring[:, 2, k * D + half * HALF:k * D + (half + 1) * HALF],
                                      start=(k == 0), stop=(k == KF - 1))
                    last.then_inc(ov_pe[l], 1)
                return tile

            def ov_ready(l):
                pe.wait_ge(y_act, (l + 1) * N_EXP)
                pe.wait_ge(y_dve, (l + 1) * N_EXP)

            pe.wait_ge(silu_c, 1)
            ada(ADA_START)
            ada(ADA_NORM)
            pe.wait_ge(in_tables, 16)
            for l in range(DEPTH):
                nq = q_tiles(l)
                if l:
                    ada(ADA_COMBINE)
                projection(l)
                n = PROJ_BEFORE[l] + len(PROJ[l])
                pe.wait_ge(proj_act, (n + 1) // 2)
                pe.wait_ge(proj_dve, n // 2)
                pe.wait_ge(qk_ready, NT * (l + 1))
                pairs(l, "A")
                pairs(l, "N")
                pairs_moved(l, "A")
                pairs_moved(l, "N")
                attention(l)
                pe.wait_ge(o_ev, UNITS_BEFORE[l] + len(UNITS[l]))
                pairs(l, "R")
                pairs_moved(l, "R")
                retention(l)
                if l == 0:
                    pe.wait_ge(ada_ev, ADA_RET[-1] + 1)
                for t in range(2):
                    rows_transposed(ROWS_BEFORE[l, "merge"] + t)
                for t in range(nq):
                    out_projection(l, t)
                    if t + 2 < nq:
                        rows_transposed(ROWS_BEFORE[l, "merge"] + t + 2)
                    if nq > 2 and t == 2:
                        rows_transposed(ROWS_BEFORE[l, "norm2"])
                pe.wait_ge(wout_mm, 2 * (NT * l + nq))
                pe.sem_inc(w_used, N_WOUT)
                for t in range(1 if nq > 2 else 0, nq):
                    rows_transposed(ROWS_BEFORE[l, "norm2"] + t)
                router(l)
                ada(ADA_LAST if l else ADA_ROUTE)
                ranks(l)
                if l == 0:
                    ada(ADA_SLOTS)
                pe.wait_ge(ada_ev, (ADA_LAST if l else ADA_SLOTS)[-1] + 1)
                moe(l)
                overflow(pe, l, ov_tile(l), lambda: ov_ready(l))

        norm_tiles = {}
        for l in range(DEPTH):
            for what in ("norm1", "norm2"):
                norm_tiles[l, what] = len(norm_tiles)
        NORMS_BEFORE = {(0, "norm1"): 0, (0, "norm2"): NT, (1, "norm1"): NT + q_tiles(0),
                        (1, "norm2"): 2 * NT + q_tiles(0), "final": 2 * NT + q_tiles(0) + q_tiles(1)}

        def h2_stored(n, parity):
            return 16 * sum(m % 2 == parity for l in range(DEPTH)
                            for m in range(ROWS_BEFORE[l, "norm2"], ROWS_BEFORE[l, "norm2"] + q_tiles(l)) if m < n)

        @block.scalar
        def _(act):
            A = nc.scalar.activation
            step = [0]

            def square_sqrt(x, dst, k):
                A(dst, x, ACT.Square, accum_out=ss[:, k:k + 1]).then_inc(row_sq, 1)
                act.wait_ge(row_sq, k + 1)
                A(rstd[:, k:k + 1], ss[:, k:k + 1], ACT.Sqrt, bias=eps[:], scale=1.0 / D).then_inc(row_std, 1)

            def norm_stat(l, what, t):
                n, k = ROWS_BEFORE[l, what] + t, NORMS_BEFORE[l, what] + t
                if what == "norm2":
                    act.wait_ge(x_upd, 2 * (NT * l + t + 1))
                elif l:
                    act.wait_ge(moe_x, sum(q_tiles(m) for m in range(l - 1)) + t + 1)
                if n >= 2:
                    act.wait_ge(rowT_mm, 2 * (n - 1))
                if h2_stored(n, n % 2):
                    act.wait_ge(h2_out[n % 2], h2_stored(n, n % 2))
                square_sqrt(X[:, t, :], rowbuf[:, n % 2, :], k)

            def rows_moved(n, t):
                act.wait_ge(rowT_mm, 2 * n + 1)
                A(T[:, 0:4, t * P:(t + 1) * P], ps[:, 2 + 2 * (n % 2), :].rearrange("p (k c) -> p k c", k=4),
                  ACT.Copy).then_inc(rowT_act, 1)

            def norm(l, what, count):
                n = ROWS_BEFORE[l, what]
                for t in range(count):
                    rows_moved(n + t, t)
                    if t + 2 < count:
                        norm_stat(l, what, t + 2)

            def attention(l):
                us, before = UNITS[l], UNITS_BEFORE[l]

                def exponentials(i):
                    n, cols = before + i, P * len(us[i]["keys"])
                    act.wait_ge(max_ready, n + 1)
                    if n >= 2:
                        act.wait_ge(pT_mm, n - 1)
                    if n >= 4:
                        act.wait_ge(o_ev, n - 3)
                    A(R2[:, 0, (n % 2) * HALF:(n % 2) * HALF + cols], ps[:, SCORE_BANK[n % 3], 0:cols], ACT.Exp,
                      bias=soft[:, 0, n % 4:n % 4 + 1], accum_out=soft[:, 1, n % 4:n % 4 + 1]).then_inc(probs_ready, 1)

                def transposed_moved(i):
                    n, cols = before + i, P * len(us[i]["keys"])
                    act.wait_ge(pT_mm, n + 1)
                    if n >= 2:
                        act.wait_ge(o_mm, n - 1)
                    A(R2[:, 1, (n % 2) * HALF:(n % 2) * HALF + cols], ps[:, 2 + n % 2, 0:cols],
                      ACT.Copy).then_inc(pT_ev, 1)

                exponentials(0)
                for i in range(len(us)):
                    if i + 1 < len(us):
                        exponentials(i + 1)
                    transposed_moved(i)

            def retention(l):
                lag, ahead = const("lag"), const("ahead")

                def decays(r):
                    head = l * N_RH + r
                    f, b = 2 * N_RH * l + r, 2 * N_RH * l + N_RH + r
                    near, far = near_tab[r % 2], far_tab[r % 2]
                    if r >= 2:
                        act.wait_ge(rscore_w, RJ_BEFORE[l] + (r - 1) * len(ret_jobs(l)))
                    A(near, ahead, ACT.Exp, scale=lg[:, 0, f:f + 1]).then_inc(decay_exp, 1)
                    A(far, lag, ACT.Exp, bias=lg[:, 2, f:f + 1], scale=lg[:, 0, f:f + 1]).then_inc(decay_exp, 1)
                    if r:
                        act.wait_ge(w_ready, head)
                    A(T[:, 6, 0:LAGS], behind, ACT.Exp, scale=lg[:, 1, b:b + 1]).then_inc(decay_exp, 1)
                    A(T[:, 7, 0:LAGS], lag, ACT.Exp, bias=lg[:, 2, b:b + 1], scale=lg[:, 1, b:b + 1]).then_inc(decay_exp, 1)

                def moved(r):
                    head, nq = l * N_RH + r, q_tiles(l)
                    act.wait_ge(ro_mm, head + 1)
                    A(z[:, 0:nq, R_Q + HD * r:R_Q + HD * (r + 1)],
                      ps[:, 7 - 2 * (head % 2), 0:nq * HD].rearrange("p (t d) -> p t d", d=HD),
                      ACT.Copy).then_inc(ro_ev, 1)

                act.wait_ge(behind_ready, l + 1)
                decays(0)
                for r in range(N_RH):
                    if r + 1 < N_RH:
                        decays(r + 1)
                    if r == 0:
                        for t in range(q_tiles(l)):
                            last = A(z[:, t, R_G:], z[:, t, R_G:], ACT.Silu)
                        last.then_inc(silu_g, 1)
                    moved(r)

            def moe(l):
                def xT_moved(e, i):
                    n = l * N_EXP + e
                    act.wait_ge(xT_mm, i * 4 + (2 * n + 1))
                    A(xgT[e % 2][:, 0:4, :], ps[:, 4, :].rearrange("p (k c) -> p k c", k=4),
                      ACT.Copy).then_inc(xT_act, 1)

                def silu(e, i):
                    n = l * N_EXP + e
                    act.wait_ge(w_used, i * RING + (moe_block(l, e, 0) + 1))
                    if n:
                        act.wait_ge(act_ready, i * 2 + n)
                    A(s1, ps[:, 0, :], ACT.Silu).then_inc(silu_h, 1)

                def aT_moved(e, i):
                    n = l * N_EXP + e
                    act.wait_ge(aT_mm, i * 2 + (n + 1))
                    A(actT[e % 2], ps[:, 6, :].rearrange("p (k c) -> p k c", k=KF), ACT.Copy).then_inc(aT_ev, 1)

                def y_moved(e, i):
                    n = l * N_EXP + e
                    act.wait_ge(y_mm, i * 2 + (n + 1))
                    if n >= 2:
                        act.wait_ge(y_out[e % 2], i * 16 + 16 * (n // 2))
                    A(ybuf[e % 2][:, 0:HALF], ps[:, 2, :], ACT.Copy).then_inc(y_act, 1)

                def turn(e, i, more=True):
                    silu(e, i)
                    y_moved(e - 1, i)
                    if more:
                        xT_moved(e + 1, i)
                    aT_moved(e, i)

                xT_moved(0, 0)
                silu(0, 0)
                xT_moved(1, 0)
                aT_moved(0, 0)
                turn(1, 0)
                turn(2, 0)
                with act.Fori(0, (N_EXP - 4) // 2) as i:
                    turn(3, i)
                    turn(4, i)
                turn(N_EXP - 1, 0, more=False)
                y_moved(N_EXP - 1, 0)

            def ov_tile(l):
                def tile(t, _):
                    act.wait_ge(ov_pe[l], 4 * t + 1)
                    A(xgT[0], ps[:, 4:6, :].rearrange("p b (k c) -> p (b k) c", k=4), ACT.Copy).then_inc(ov_act[l], 1)
                    act.wait_ge(ov_pe[l], 4 * t + 2)
                    A(s1, ps[:, 0, :], ACT.Silu).then_inc(ov_act[l], 1)
                    act.wait_ge(ov_pe[l], 4 * t + 3)
                    A(actT[0], ps[:, 6, :].rearrange("p (k c) -> p k c", k=KF), ACT.Copy).then_inc(ov_act[l], 1)
                    act.wait_ge(ov_pe[l], 4 * t + 4)
                    A(ybuf[0].rearrange("p (b c) -> p b c", b=2), ps[:, 2:4, :], ACT.Copy).then_inc(ov_act[l], 1)
                return tile

            def combine(l, tiles):
                for t in tiles:
                    act.wait_ge(yg_in[t % 2], 32 * (sum(q_tiles(m) for m in range(l)) // 2 + t // 2 + 1))
                    A(yg[t % 2][:, 0, :], yg[t % 2][:, 0, :], ACT.Copy, scale=rw[:, t, 0:1]).then_inc(comb_mul, 1)

            act.dma_start(lg[:, 3, :], g["ret_decay"].rearrange("l s h -> (l s h)").partition_broadcast(P)).then_inc(in_decay, 16)
            act.dma_start(C[:], g["consts"]).then_inc(in_tables, 16)
            for t in range(NT):
                src = g["x"][0, t * P:(t + 1) * P] if t < LT else g["ctx"][0, (t - LT) * P:(t - LT + 1) * P]
                act.dma_start(X[:, t, :], src).then_inc(in_x, 16)
            act.wait_ge(in_c, 32)
            A(c_col[:].rearrange("p k s -> p s k"), c_raw[:], ACT.Silu).then_inc(silu_c, 1)
            act.wait_ge(decay_u, 1)
            A(lgt[:, 0, :], lgt[:, 0, :], ACT.Exp, scale=-1.0).then_inc(decay_u, 1)
            act.wait_ge(in_x, 16 * NT)
            act.wait_ge(eps_set, 1)
            for l in range(DEPTH):
                nq = q_tiles(l)
                if l:
                    combine(0, (0, 1))
                    norm_stat(l, "norm1", 0)
                    combine(0, (2,))
                    norm_stat(l, "norm1", 1)
                    combine(0, (3,))
                else:
                    norm_stat(l, "norm1", 0)
                    norm_stat(l, "norm1", 1)
                norm(l, "norm1", NT)
                std_after = next(i for i, (n, _) in enumerate(PROJ[l]) if n == 2)
                for i, (n, t) in enumerate(PROJ[l]):
                    job = PROJ_BEFORE[l] + i
                    if i == std_after:
                        act.wait_ge(qk_ss, NT * (l + 1))
                        A(hr[:, :, 0:8], hss[:, :, 0:8], ACT.Sqrt, bias=eps[:], scale=1.0 / HD).then_inc(qk_std, 1)
                    if job % 2 == 0:
                        act.wait_ge(proj_mm, job + 1)
                        for lo, hi in needed(l, t, n):
                            last = A(z[:, t, n * HALF + lo:n * HALF + hi], ps[:, PROJ_BANKS[job % 4], lo:hi], ACT.Copy)
                        last.then_inc(proj_act, 1)

                def pairs_moved(group):
                    for i, (_, is_q) in enumerate(PAIRS[group]):
                        job = l * N_PAIRS + PAIR_FIRST[group] + i
                        if job % 2 == 0:
                            cols = P * (nq if is_q else NT)
                            act.wait_ge(pair_mm, job + 1)
                            A(T[:, PAIR_SLOT[group] + i, 0:cols], ps[:, 2 + job % 4, 0:cols], ACT.Copy,
                              scale=HD ** -0.5 if group == "N" and is_q else 1.0).then_inc(pair_act, 1)

                pairs_moved("A")
                pairs_moved("N")
                attention(l)
                pairs_moved("R")
                retention(l)
                merged = sum(q_tiles(m) for m in range(l))
                act.wait_ge(ro_ev, (l + 1) * N_RH)
                act.wait_ge(o_ev, UNITS_BEFORE[l] + len(UNITS[l]))

                def merge_squares(t):
                    sq = T[:, 2 * t:2 * t + 2, :].rearrange("p a b -> p (a b)")
                    for c0, d0, w in MERGED:
                        last = A(sq[:, d0:d0 + w], z[:, t, c0:c0 + w], ACT.Square)
                    last.then_inc(mg_sq, 1)

                merge_squares(0)
                for t in range(nq):
                    if t + 1 < nq:
                        merge_squares(t + 1)
                    act.wait_ge(mg_ss, merged + t + 1)
                    A(hr[:, t, :], hss[:, t, :], ACT.Sqrt, bias=eps[:], scale=1.0 / HD).then_inc(mg_std, 1)
                for t in range(nq):
                    rows_moved(ROWS_BEFORE[l, "merge"] + t, t)
                norm_stat(l, "norm2", 0)
                norm_stat(l, "norm2", 1)
                norm(l, "norm2", nq)
                act.wait_ge(rt_max, l + 1)
                A(rtmp[:, 0:nq * N_EXP], rtmp[:, 0:nq * N_EXP], ACT.Exp).then_inc(rt_exp, 1)
                moe(l)
                overflow(act, l, ov_tile(l), lambda: act.wait_ge(y_out[1], 16 * (l + 1) * N_EXP // 2))
            for t in range(LT):
                combine(1, (t,))
            for t in range(LT):
                act.wait_ge(moe_x, q_tiles(0) + t + 1)
                square_sqrt(X[:, t, :], rowbuf[:, t, :], NORMS_BEFORE["final"] + t)

        @block.vector
        def _(dve):
            V = nc.vector
            step = [0]

            def link(ins):
                step[0] += 1
                ins.then_inc(dve_step, 1)
                dve.wait_ge(dve_step, step[0])

            def tt(o, a, b, op):
                return V.tensor_tensor(o, a, b, op)

            def heads(ap):
                return ap.rearrange("p (h d) -> p h d", d=HD)

            def norm_rows(k, streams):
                dve.wait_ge(in_rows, 16 * ROW_LOADS[k])
                for s in range(streams):
                    link(V.scalar_tensor_tensor(out=rows[2 * s], in0=rows[2 * s], scalar=1.0, in1=rows[4],
                                                op0=ALU.add, op1=ALU.mult))

            def norm_row(l, what, t):
                n, k, s = ROWS_BEFORE[l, what] + t, NORMS_BEFORE[l, what] + t, t // LT
                dve.wait_ge(row_std, k + 1)
                link(V.reciprocal(rstd[:, k:k + 1], rstd[:, k:k + 1]))
                link(V.scalar_tensor_tensor(out=rowbuf[:, n % 2, :], in0=X[:, t, :], scalar=rstd[:, k:k + 1],
                                            in1=rows[2 * s], op0=ALU.mult, op1=ALU.mult))
                tt(rowbuf[:, n % 2, :], rowbuf[:, n % 2, :], rows[2 * s + 1], ALU.add).then_inc(row_ready, 1)

            def rows_moved(n, t):
                dve.wait_ge(rowT_mm, 2 * n + 2)
                V.tensor_copy(T[:, 4:8, t * P:(t + 1) * P],
                              ps[:, 3 + 2 * (n % 2), :].rearrange("p (k c) -> p k c", k=4)).then_inc(rowT_dve, 1)

            def ada_moved(jobs, bank0=0):
                for job in jobs:
                    dve.wait_ge(in_brow[job % 2], 16 * (job // 2 + 1))
                    dve.wait_ge(w_used, ADA_BLOCK[job] + 1)
                    tt(modrow(job), ps[0:2, bank0 + job % 2, :], modrow(job), ALU.add).then_inc(ada_ev, 1)

            def qk_squares(l, t):
                h0 = 0 if t < q_tiles(l) else 6
                sq = R2[:, 0, HD * h0:HALF]
                link(tt(sq, z[:, t, HD * h0:HALF], z[:, t, HD * h0:HALF], ALU.mult))
                V.tensor_reduce(hss[:, t, h0:8], heads(sq), X_AXIS, ALU.add).then_inc(qk_ss, 1)
                dve.wait_ge(qk_ss, NT * l + t + 1)

            def qk_norm(l, t):
                h0 = 0 if t < q_tiles(l) else 6
                v, normed = z[:, t, HD * h0:HALF], R2[:, 0, HD * h0:HALF]
                link(tt(heads(normed), heads(v), hr[:, t, h0:8].unsqueeze(2).to_broadcast([P, 8 - h0, HD]), ALU.mult))
                if h0 == 0:
                    link(tt(z[:, t, 0:A_K].rearrange("p (i g d) -> p g i d", g=2, d=HD),
                            R2[:, 0, 0:A_K].rearrange("p (g i d) -> p g i d", g=2, d=HD),
                            qk_gain[:, l, 0, :].unsqueeze(1).unsqueeze(1).to_broadcast([P, 2, 3, HD]), ALU.mult))
                ins = tt(heads(z[:, t, A_K:A_V]), heads(R2[:, 0, A_K:A_V]),
                         qk_gain[:, l, 1, :].unsqueeze(1).to_broadcast([P, 2, HD]), ALU.mult)
                if t < LT:
                    link(ins)
                    cos, sin = const("cos")[:, HD * t:HD * (t + 1)], const("sin")[:, HD * t:HD * (t + 1)]
                    by_cos, by_sin = R2[:, 0, 0:HALF], R2[:, 0, HALF:]
                    link(tt(heads(by_cos), heads(v), cos.unsqueeze(1).to_broadcast([P, 8, HD]), ALU.mult))
                    zv, sv = (x.rearrange("p (h f j i) -> p h f j i", h=8, f=2, j=2) for x in (v, by_sin))
                    sn = sin.rearrange("p (f j i) -> p f j i", f=2, j=2)
                    for j in range(2):
                        link(tt(sv[:, :, :, j, :], zv[:, :, :, 1 - j, :],
                                sn[:, :, j, :].unsqueeze(1).to_broadcast([P, 8, 2, 16]), ALU.mult))
                    ins = tt(v, by_cos, by_sin, ALU.add)
                ins.then_inc(qk_ready, 1)
                dve.wait_ge(qk_ready, NT * l + t + 1)

            def projection(l):
                first = {n: next(i for i, (m, _) in enumerate(PROJ[l]) if m == n) for n in range(N_WIN)}
                for i, (n, t) in enumerate(PROJ[l]):
                    job = PROJ_BEFORE[l] + i
                    if i == first[2]:
                        dve.wait_ge(proj_act, (PROJ_BEFORE[l] + first[1] + 1) // 2)
                        for tile in range(NT):
                            qk_squares(l, tile)
                    if i == first[3]:
                        dve.wait_ge(qk_std, l + 1)
                        link(V.reciprocal(hr[:, :, 0:8], hr[:, :, 0:8]))
                        for tile in range(LT):
                            qk_norm(l, tile)
                    if i == first[4]:
                        for tile in range(LT, NT):
                            qk_norm(l, tile)
                    if job % 2 == 1:
                        dve.wait_ge(proj_mm, job + 1)
                        for lo, hi in needed(l, t, n):
                            last = V.tensor_copy(z[:, t, n * HALF + lo:n * HALF + hi], ps[:, PROJ_BANKS[job % 4], lo:hi])
                        last.then_inc(proj_dve, 1)

            def bias(l):
                dve.wait_ge(in_bias, 16 * 16 * (l + 1))
                v = R3[:].rearrange("p a b -> p (a b)").rearrange("p (n k) -> p n k", k=GRID_W)
                tt(v, v, const("mask").unsqueeze(1).to_broadcast([P, 32, GRID_W]), ALU.add).then_inc(bias_ready, 1)

            def pairs_moved(l, group):
                for i, (_, is_q) in enumerate(PAIRS[group]):
                    job = l * N_PAIRS + PAIR_FIRST[group] + i
                    if job % 2 == 1:
                        cols = P * (q_tiles(l) if is_q else NT)
                        dve.wait_ge(pair_mm, job + 1)
                        o, src = T[:, PAIR_SLOT[group] + i, 0:cols], ps[:, 2 + job % 4, 0:cols]
                        if group == "N" and is_q:
                            V.tensor_scalar(o, src, HD ** -0.5, None, ALU.mult).then_inc(pair_dve, 1)
                        else:
                            V.tensor_copy(o, src).then_inc(pair_dve, 1)

            def attention(l):
                us, before = UNITS[l], UNITS_BEFORE[l]

                def maximum(i):
                    n, cols = before + i, P * len(us[i]["keys"])
                    dve.wait_ge(score_mm, n + 1)
                    V.tensor_reduce(soft[:, 0, n % 4:n % 4 + 1], ps[:, SCORE_BANK[n % 3], 0:cols], X_AXIS, ALU.max,
                                    negate=True).then_inc(max_ready, 1)

                def output(i):
                    u, n = us[i], before + i
                    dve.wait_ge(o_mm, n + 1)
                    link(V.reciprocal(soft[:, 2, n % 4:n % 4 + 1], soft[:, 1, n % 4:n % 4 + 1]))
                    V.tensor_scalar(z[:, u["t"], u["o"]:u["o"] + HD], ps[:, 4 + n % 2, 0:HD],
                                    soft[:, 2, n % 4:n % 4 + 1], None, ALU.mult).then_inc(o_ev, 1)

                maximum(0)
                maximum(1)
                for i in range(len(us) + 1):
                    if i + 2 < len(us):
                        maximum(i + 2)
                    if i >= 1:
                        output(i - 1)

            def retention(l):
                jobs, nj = ret_jobs(l), len(ret_jobs(l))

                def tables(r):
                    head = l * N_RH + r
                    near, far = near_tab[r % 2], far_tab[r % 2]
                    dve.wait_ge(decay_exp, 4 * (head + 1))
                    link(tt(near, near, T[:, 6, 0:LAGS], ALU.mult))
                    link(tt(far, far, T[:, 7, 0:LAGS], ALU.add))
                    tt(near[:, P:2 * P], near[:, P:2 * P], ident, ALU.add).then_inc(w_ready, 1)
                    dve.wait_ge(w_ready, head + 1)

                def windows(r, table):
                    v = (near_tab if table == "near" else far_tab)[r % 2][:, 0:256]
                    return bass.AP(v.tensor, v.offset, [v.ap[0], [P, 2], [1, 256]])

                def weighted(r):
                    for j, (_, _, table) in enumerate(jobs):
                        job = RJ_BEFORE[l] + r * nj + j
                        dve.wait_ge(rscore_mm, job + 1)
                        before = r * nj + j - 4
                        if before >= 0:
                            dve.wait_ge(ro_mm, l * N_RH + before // nj + 1)
                        o = R2[:, (job % 4) // 2, (job % 2) * HALF:(job % 2 + 1) * HALF]
                        V.scalar_tensor_tensor(out=o.rearrange("p (k c) -> p k c", k=2),
                                               in0=ps[:, RET_BANK[j], :].rearrange("p (k c) -> p k c", k=2),
                                               scalar=HD ** -0.5, in1=windows(r, table), op0=ALU.mult, op1=ALU.mult).then_inc(rscore_w, 1)
                    dve.wait_ge(rscore_w, RJ_BEFORE[l] + (r + 1) * nj)

                tables(0)
                for r in range(N_RH):
                    if r + 1 < N_RH:
                        tables(r + 1)
                    weighted(r)
                    if l == 0:
                        ada_moved([ADA_RET[r]], 2)

            def merge_sums(l, t):
                n = sum(q_tiles(m) for m in range(l)) + t
                dve.wait_ge(mg_sq, n + 1)
                sq = T[:, 2 * t:2 * t + 2, :].rearrange("p a b -> p (a b)")
                V.tensor_reduce(hss[:, t, :], heads(sq), X_AXIS, ALU.add).then_inc(mg_ss, 1)

            def merge_row(l, t):
                n = ROWS_BEFORE[l, "merge"] + t
                row = rowbuf[:, n % 2, :]
                dve.wait_ge(rowT_mm, 2 * (n - 1))
                dve.wait_ge(mg_std, sum(q_tiles(m) for m in range(l)) + t + 1)
                link(V.reciprocal(hr[:, t, :], hr[:, t, :]))
                for c0, d0, w in MERGED:
                    link(tt(heads(row[:, d0:d0 + w]), heads(z[:, t, c0:c0 + w]),
                            hr[:, t, d0 // HD:(d0 + w) // HD].unsqueeze(2).to_broadcast([P, w // HD, HD]), ALU.mult))
                link(tt(row, row, R3[:, 0, :], ALU.mult))
                tt(row[:, 640:], row[:, 640:], z[:, t, R_G:], ALU.mult).then_inc(row_ready, 1)

            def x_update(l, t):
                for half in range(2):
                    job = 2 * (NT * l + t) + half
                    tmp, cols = R3[:, 1, half * HALF:(half + 1) * HALF], slice(half * HALF, (half + 1) * HALF)
                    dve.wait_ge(wout_mm, job + 1)
                    link(tt(tmp, ps[:, 6 + half, :], R1[:, t // LT, cols], ALU.mult))
                    tt(X[:, t, cols], X[:, t, cols], tmp, ALU.add).then_inc(x_upd, 1)
                dve.wait_ge(x_upd, 2 * (NT * l + t) + 2)

            def routing(l):
                nq = q_tiles(l)
                w = nq * N_EXP
                free = [w]

                def new(cols):
                    a = free[0]
                    free[0] += cols
                    return rtmp[:, a:a + cols]

                def by(ap, k):
                    return ap.rearrange("p (n e) -> p n e", e=k)

                def wide(ap, k):
                    return ap.unsqueeze(2).to_broadcast([P, ap.shape[1], k])

                def reduce(v, k, op):
                    o = new(v.shape[1] // k)
                    link(V.tensor_reduce(o, by(v, k), X_AXIS, op))
                    return o

                def first_of_max(v, k, order):
                    top = reduce(v, k, ALU.max)
                    at, o = new(v.shape[1]), new(v.shape[1])
                    link(tt(by(at, k), by(v, k), wide(top, k), ALU.is_equal))
                    link(tt(by(at, k), by(at, k), order.unsqueeze(1).to_broadcast([P, v.shape[1] // k, k]), ALU.mult))
                    lead = reduce(at, k, ALU.max)
                    link(tt(by(o, k), by(at, k), wide(lead, k), ALU.is_equal))
                    return o, top

                dve.wait_ge(rt_mm, l + 1)
                p = rtmp[:, 0:w]
                link(tt(by(p, N_EXP), ps[:, 6, 0:w].rearrange("p (n e) -> p n e", e=N_EXP),
                        b_rt[:].unsqueeze(1).to_broadcast([P, nq, N_EXP]), ALU.add))
                m = reduce(p, N_EXP, ALU.max)
                tt(by(p, N_EXP), by(p, N_EXP), wide(m, N_EXP), ALU.subtract).then_inc(rt_max, 1)
                dve.wait_ge(rt_exp, l + 1)
                s = reduce(p, N_EXP, ALU.add)
                link(V.reciprocal(s, s))
                link(tt(by(p, N_EXP), by(p, N_EXP), wide(s, N_EXP), ALU.mult))
                g4 = p.rearrange("p (n i) -> p n i", i=4)
                hi1, lo1, hi2, lo2 = (new(nq * 4) for _ in range(4))
                link(tt(hi1, g4[:, :, 0], g4[:, :, 1], ALU.max))
                link(tt(lo1, g4[:, :, 0], g4[:, :, 1], ALU.min))
                link(tt(hi2, g4[:, :, 2], g4[:, :, 3], ALU.max))
                link(tt(lo2, g4[:, :, 2], g4[:, :, 3], ALU.min))
                link(tt(lo1, lo1, lo2, ALU.max))
                link(tt(lo2, hi1, hi2, ALU.min))
                link(tt(hi1, hi1, hi2, ALU.max))
                link(tt(lo1, lo1, lo2, ALU.max))
                link(tt(hi1, hi1, lo1, ALU.add))
                chosen, _ = first_of_max(hi1, 4, const("down")[:, 0:4])
                cand = new(w)
                link(tt(by(cand, 4), g4, wide(chosen, 4), ALU.mult))
                oh1, m1 = first_of_max(cand, N_EXP, const("down"))
                link(V.scalar_tensor_tensor(out=cand, in0=oh1, scalar=-2.0, in1=cand, op0=ALU.mult, op1=ALU.add))
                oh2, m2 = first_of_max(cand, N_EXP, const("down"))
                link(tt(rtmp[:, 0:w], oh1, oh2, ALU.add))
                s2 = new(nq)
                link(tt(s2, m1, m2, ALU.add))
                link(V.reciprocal(s2, s2))
                link(tt(rw[:, 0:nq, 0], m1, s2, ALU.mult))
                tt(rw[:, 0:nq, 1], m2, s2, ALU.mult).then_inc(rt_sel, 1)
                return oh1, oh2, new, by, reduce

            def slot_numbers(l, oh1, oh2, new, by, reduce):
                nq = q_tiles(l)
                w = nq * N_EXP
                dve.wait_ge(rank_mm, l + 1)
                rank, q, t1, ge1 = (new(w + N_EXP) for _ in range(4))
                link(V.tensor_copy(rank, ps[:, 7, 0:w + N_EXP]))
                link(V.tensor_scalar(rank[:, w:], rank[:, w:], -1.0, None, ALU.add))
                link(V.tensor_scalar(ge1, rank, 128.0, None, ALU.is_ge))
                link(V.tensor_scalar(q, rank, 256.0, None, ALU.is_ge))
                link(V.tensor_scalar(t1, rank, 384.0, None, ALU.is_ge))
                link(tt(q, q, t1, ALU.add))
                link(tt(q, q, ge1, ALU.add))
                a, b = new(N_EXP), new(N_EXP)
                link(V.tensor_copy(a, q[:, w:]))
                for s in (1, 2, 4, 8):
                    link(V.tensor_copy(b[:, 0:s], a[:, 0:s]))
                    link(tt(b[:, s:], a[:, s:], a[:, 0:N_EXP - s], ALU.add))
                    a, b = b, a
                base = new(N_EXP)
                link(tt(base, a, q[:, w:], ALU.subtract))
                link(V.scalar_tensor_tensor(out=base, in0=base, scalar=15.0, in1=const("up"), op0=ALU.add, op1=ALU.subtract))
                addr = rank[:, 0:w]
                link(V.tensor_scalar(addr, addr, float(SLOT_T[l]), None, ALU.mult))
                link(V.scalar_tensor_tensor(out=addr, in0=q[:, 0:w], scalar=1.0 - SLOT_T[l] * P, in1=addr,
                                            op0=ALU.mult, op1=ALU.add))
                every = [P, nq, N_EXP]
                link(tt(by(ge1[:, 0:w], N_EXP), by(ge1[:, 0:w], N_EXP), base.unsqueeze(1).to_broadcast(every), ALU.mult))
                link(tt(addr, addr, ge1[:, 0:w], ALU.add))
                link(tt(by(addr, N_EXP), by(addr, N_EXP), const("up").unsqueeze(1).to_broadcast(every), ALU.add))
                for k, oh in enumerate((oh1, oh2)):
                    link(tt(oh, oh, addr, ALU.mult))
                    s = reduce(oh, N_EXP, ALU.add)
                    link(V.tensor_copy(slots[:, 0:nq, k], s))
                n_ov, over = OV_MAX[0], new(OV_MAX[0] * N_EXP)
                v = over[0:1, :].rearrange("p (t e) -> p t e", e=N_EXP)
                link(tt(v, a[0:1, :].unsqueeze(1).to_broadcast([1, n_ov, N_EXP]),
                        const("up")[0:1, 0:n_ov].unsqueeze(2).to_broadcast([1, n_ov, N_EXP]), ALU.is_le))
                e = new(TOP)
                link(V.tensor_reduce(e[0:1, 1:TOP], v, X_AXIS, ALU.add))
                link(V.tensor_scalar(e[0:1, 1:TOP], e[0:1, 1:TOP], float(N_EXP - 1), None, ALU.min))
                link(V.tensor_copy(e[0:1, 0:1], a[0:1, N_EXP - 1:N_EXP]))
                V.tensor_copy(ovinfo[:], e[0:1, :]).then_inc(slots_ready, 1)

            def moe(l):
                def xT_moved(e, i):
                    n = l * N_EXP + e
                    dve.wait_ge(xT_mm, i * 4 + (2 * n + 2))
                    V.tensor_copy(xgT[e % 2][:, 4:8, :],
                                  ps[:, 5, :].rearrange("p (k c) -> p k c", k=4)).then_inc(xT_dve, 1)

                def gated(e, i):
                    n = l * N_EXP + e
                    dve.wait_ge(w_used, i * RING + (moe_block(l, e, 1) + 1))
                    dve.wait_ge(silu_h, i * 2 + (n + 1))
                    if n:
                        dve.wait_ge(aT_mm, i * 2 + n)
                    tt(act_sb, s1, ps[:, 1, :], ALU.mult).then_inc(act_ready, 1)

                def y_moved(e, i):
                    n = l * N_EXP + e
                    dve.wait_ge(w_used, i * RING + (moe_block(l, e, 2) + 1))
                    if n >= 2:
                        dve.wait_ge(y_out[e % 2], i * 16 + 16 * (n // 2))
                    V.tensor_copy(ybuf[e % 2][:, HALF:], ps[:, 3, :]).then_inc(y_dve, 1)

                def turn(e, i, more=True):
                    y_moved(e - 1, i)
                    gated(e, i)
                    if more:
                        xT_moved(e + 1, i)

                xT_moved(0, 0)
                gated(0, 0)
                xT_moved(1, 0)
                turn(1, 0)
                turn(2, 0)
                with dve.Fori(0, (N_EXP - 4) // 2) as i:
                    turn(3, i)
                    turn(4, i)
                turn(N_EXP - 1, 0, more=False)
                y_moved(N_EXP - 1, 0)

            def ov_tile(l):
                def tile(t, _):
                    dve.wait_ge(ov_act[l], 4 * t + 2)
                    tt(act_sb, s1, ps[:, 1, :], ALU.mult).then_inc(ov_dve[l], 1)
                return tile

            def combine(l, tiles):
                done = sum(q_tiles(m) for m in range(l))
                dve.wait_ge(in_gate, 32 * (2 * l + 2))
                for t in tiles:
                    dve.wait_ge(comb_mul, done + t + 1)
                    y0, y1 = yg[t % 2][:, 0, :], yg[t % 2][:, 1, :]
                    link(V.scalar_tensor_tensor(out=y0, in0=y1, scalar=rw[:, t, 1:2], in1=y0, op0=ALU.mult, op1=ALU.add))
                    link(tt(y0, y0, R1[:, t // LT, :], ALU.mult))
                    tt(X[:, t, :], X[:, t, :], y0, ALU.add).then_inc(moe_x, 1)

            V.memset(R3[0:120, 0, 0:P], 0.0).then_inc(pad_zero, 1)
            V.memset(hss[:], 1.0).then_inc(pad_zero, 1)
            V.memset(eps[:], EPS).then_inc(eps_set, 1)
            nl = 2 * DEPTH * N_RH
            dve.wait_ge(in_decay, 16)
            x, t0, t1, acc = lg[:, 3, :], lgt[:, 0, :], lgt[:, 1, :], lg[:, 0, :]
            link(V.tensor_scalar(t0, x, -1.0, None, ALU.mult))
            tt(t0, t0, x, ALU.max).then_inc(decay_u, 1)
            dve.wait_ge(decay_u, 2)
            link(V.tensor_scalar(t1, t0, 2.0, None, ALU.add))
            link(V.reciprocal(t1, t1))
            link(tt(t0, t0, t1, ALU.mult))
            link(tt(t1, t0, t0, ALU.mult))
            link(V.memset(acc, 0.0))
            for n in range(17, 1, -2):
                link(V.scalar_tensor_tensor(out=acc, in0=acc, scalar=1.0 / n, in1=t1, op0=ALU.add, op1=ALU.mult))
            link(V.scalar_tensor_tensor(out=acc, in0=acc, scalar=1.0, in1=t0, op0=ALU.add, op1=ALU.mult))
            link(V.tensor_scalar(x, x, 0.0, None, ALU.min))
            link(V.scalar_tensor_tensor(out=acc, in0=acc, scalar=-2.0, in1=x, op0=ALU.mult, op1=ALU.add))
            link(V.tensor_scalar(lg[:, 1, :], acc, -1.0, None, ALU.mult))
            link(V.tensor_scalar(lg[:, 2, :], acc, 256.0, None, ALU.mult))
            ada_moved(ADA_START)
            for l in range(DEPTH):
                nq = q_tiles(l)
                n = ROWS_BEFORE[l, "norm1"]
                if l == 0:
                    ada_moved(ADA_NORM)
                    norm_rows(0, 2)
                    norm_row(l, "norm1", 0)
                    norm_row(l, "norm1", 1)
                    dve.wait_ge(in_tables, 16)
                    dve.wait_ge(in_const, 16 * N_CONST_LOADS)
                    link(V.tensor_scalar(qk_gain[:, :, 0, :], qk_gain[:, :, 0, :], HD ** -0.5, None, ALU.mult))
                else:
                    combine(0, (0, 1))
                    ada_moved(ADA_COMBINE[0:1])
                    norm_rows(2, 2)
                    norm_row(l, "norm1", 0)
                    combine(0, (2,))
                    norm_row(l, "norm1", 1)
                    combine(0, (3,))
                    ada_moved(ADA_COMBINE[1:])
                for t in range(NT):
                    rows_moved(n + t, t)
                    if t + 2 < NT:
                        norm_row(l, "norm1", t + 2)
                projection(l)
                bias(l)
                V.tensor_scalar(behind, const("lag"), 0.0, None, ALU.min).then_inc(behind_ready, 1)
                pairs_moved(l, "A")
                pairs_moved(l, "N")
                attention(l)
                pairs_moved(l, "R")
                retention(l)
                dve.wait_ge(ro_ev, (l + 1) * N_RH)
                dve.wait_ge(o_ev, UNITS_BEFORE[l] + len(UNITS[l]))
                if l == 0:
                    for i in range(2):
                        dve.wait_ge(mod_out[i], 16 * (ADA_RET[-1] + 1) // 2)
                n = ROWS_BEFORE[l, "merge"]
                n2 = ROWS_BEFORE[l, "norm2"]
                merge_sums(l, 0)
                dve.wait_ge(silu_g, l + 1)
                dve.wait_ge(in_mix, 16 * (l + 1))
                merge_row(l, 0)
                for t in range(1, nq):
                    merge_sums(l, t)
                merge_row(l, 1)
                rows_moved(n, 0)
                rows_moved(n + 1, 1)
                for t in range(2, nq):
                    merge_row(l, t)
                dve.wait_ge(in_gate, 32 * (2 * l + 1))
                x_update(l, 0)
                if nq > 2:
                    rows_moved(n + 2, 2)
                    x_update(l, 1)
                    rows_moved(n + 3, 3)
                norm_rows(2 * l + 1, nq // LT)
                norm_row(l, "norm2", 0)
                x_update(l, nq - 2 if nq > 2 else 1)
                norm_row(l, "norm2", 1)
                if nq > 2:
                    x_update(l, 3)
                for t in range(nq):
                    rows_moved(n2 + t, t)
                    if t + 2 < nq:
                        norm_row(l, "norm2", t + 2)
                parts = routing(l)
                ada_moved(ADA_LAST if l else ADA_ROUTE)
                slot_numbers(l, *parts)
                if l == 0:
                    ada_moved(ADA_SLOTS)
                moe(l)
                overflow(dve, l, ov_tile(l), lambda: dve.nop())
            combine(1, range(LT))
            dve.wait_ge(fin_in, 16)
            for t in range(LT):
                k = NORMS_BEFORE["final"] + t
                dve.wait_ge(row_std, k + 1)
                link(V.reciprocal(rstd[:, k:k + 1], rstd[:, k:k + 1]))
                V.scalar_tensor_tensor(out=rowbuf[:, t, :], in0=X[:, t, :], scalar=rstd[:, k:k + 1], in1=R3[:, 0, :],
                                       op0=ALU.mult, op1=ALU.mult).then_inc(fin_ready, 1)

        @block.gpsimd
        def _(pool):
            dma = pool.dma_start

            def bcast(ap, n=P):
                return ap.partition_broadcast(n)

            def brow(job):
                src = g["b_ada"][job // N_ADA, (job % N_ADA) * HALF:(job % N_ADA + 1) * HALF]
                dma(modrow(job), bcast(src, 2)).then_inc(in_brow[job % 2], 16)

            def modulation_out(jobs):
                for job in jobs:
                    pool.wait_ge(ada_ev, job + 1)
                    l, n = job // N_ADA, job % N_ADA
                    dma(mod_d[l, :, n * HALF:(n + 1) * HALF], modrow(job)).then_inc(mod_out[job % 2], 16)
                    pool.wait_ge(mod_out[job % 2], 16 * (job // 2 + 1))
                    if any(first <= job and job + 2 < end for first, end in ADA_RUNS):
                        brow(job + 2)

            def norm_rows(l, k, streams):
                for s in range(streams):
                    dma(rows[2 * s], bcast(mod_d[l, s, (3 * k + 1) * D:(3 * k + 2) * D])).then_inc(in_rows, 16)
                    dma(rows[2 * s + 1], bcast(mod_d[l, s, 3 * k * D:(3 * k + 1) * D])).then_inc(in_rows, 16)
                dma(rows[4], bcast(g["norm2_g" if k else "norm1_g"][l])).then_inc(in_rows, 16)

            def gates(l, k):
                for s in range(2):
                    dma(R1[:, s, :], bcast(mod_d[l, s, (3 * k + 2) * D:(3 * k + 3) * D])).then_inc(in_gate, 16)

            def bias(l):
                v = R3[:].rearrange("p a b -> p (a b)").rearrange("p (h t k c) -> p h t k c", h=4, t=2, c=GRID_W)
                for t in range(2):
                    for r in range(2):
                        for h in range(4):
                            row = (l * 4 + h) * 15 + 7 - (2 * t + r)
                            dma(v[r * GRID_W:(r + 1) * GRID_W, h, t],
                                near_d[row:row + 4].rearrange("k q c -> q k c")).then_inc(in_bias, 16)

            brow(0)
            brow(1)
            dma(ids[:], g["ids"]).then_inc(in_const, 16)
            dma(w_rt[:], g["w_router"].rearrange("(p k) e -> p k e", k=KD)).then_inc(in_const, 16)
            dma(b_rt[:], bcast(g["b_router"])).then_inc(in_const, 16)
            for l in range(DEPTH):
                dma(qk_gain[:, l, 0, :], bcast(g["q_norm_g"][l])).then_inc(in_const, 16)
                dma(qk_gain[:, l, 1, :], bcast(g["k_norm_g"][l])).then_inc(in_const, 16)
            modulation_out(ADA_START)
            norm_rows(0, 0, 2)
            modulation_out(ADA_NORM)
            pool.wait_ge(row_ready, NT)
            pool.wait_ge(pad_zero, 1)
            dma(R3[0:120, 0, 48:79], g["na_rpb"].rearrange("l h r c -> (l h r) c")).then_inc(in_rpb, 16)
            pool.wait_ge(in_rpb, 16)
            dma(rpb_d, R3[0:120, 0, 0:P]).then_inc(rpb_out, 16)
            pool.wait_ge(in_const, 16 * N_CONST_LOADS)
            for l in range(DEPTH):
                dma(slot_d[l].rearrange("(p n) o -> p (n o)", n=SLOT_T[l]), ids[:, 0:SLOT_T[l]]).then_inc(slot_zero, 16)
            pool.wait_ge(rpb_out, 16)
            for l in range(DEPTH):
                src = bass.AP(rpb_d.tensor, l * 60 * P + 63, [[P, 60], [-1, GRID_W], [1, GRID_W]])
                dma(near_d[l * 60:(l + 1) * 60], src).then_inc(bias_spread, 16)
            for l in range(DEPTH):
                nq = q_tiles(l)
                pool.wait_ge(bias_spread, 32)
                bias(l)
                for t in range(OV_MAX[l]):
                    dma(y_d[l].rearrange("(p n) d -> p n d", n=SLOT_T[l])[:, N_EXP + t, :], g["zeros"]).then_inc(y_zero, 16)
                pool.wait_ge(score_mm, UNITS_BEFORE[l] + len(UNITS[l]))
                if l == 0:
                    brow(ADA_RET[0])
                    brow(ADA_RET[1])
                dma(R3[:, 0, :], bcast(g["mix_g"][l])).then_inc(in_mix, 16)
                if l == 0:
                    modulation_out(ADA_RET)
                pool.wait_ge(rscore_w, RJ_BEFORE[l] + N_RH * len(ret_jobs(l)))
                gates(l, 0)
                pool.wait_ge(row_ready, ROWS_BEFORE[l, "norm2"])
                norm_rows(l, 1, nq // LT)
                for t in range(nq):
                    n = ROWS_BEFORE[l, "norm2"] + t
                    pool.wait_ge(row_ready, n + 1)
                    dma(h2_d[l][t * P:(t + 1) * P], rowbuf[:, n % 2, :]).then_inc(h2_out[n % 2], 16)
                for job in (ADA_LAST if l else ADA_ROUTE)[0:2]:
                    brow(job)
                if l == 0:
                    gates(0, 1)
                pool.wait_ge(rt_mm, l + 1)
                for i in range(2):
                    pool.wait_ge(h2_out[i], h2_stored(ROWS_BEFORE[l, "norm2"] + nq, i))
                modulation_out(ADA_LAST if l else ADA_ROUTE)

                pool.wait_ge(slots_ready, l + 1)
                pool.wait_ge(slot_zero, 32)
                for t in range(nq):
                    for k in range(2):
                        pool.indirect_dma_start(slot_d[l], bass.IndirectOffsetOnAxis(ap=slots[:, t, k:k + 1], axis=0),
                                                ids[:, SLOT_T[0] + t:SLOT_T[0] + t + 1], None).then_inc(slot_out, 16)
                pool.wait_ge(slot_out, 32 * (nq + (q_tiles(0) if l else 0)))
                dma(slot_tok[:, 0:SLOT_T[l]], slot_d[l].rearrange("(p n) o -> p (n o)", n=SLOT_T[l])).then_inc(slot_in, 16)
                pool.wait_ge(slot_in, 16 * (l + 1))

                def gather(n, dst, s):
                    pool.indirect_dma_start(dst, None, h2_d[l],
                                            bass.IndirectOffsetOnAxis(ap=slot_tok[:, n:n + 1], axis=0)).then_inc(s, 16)

                y_rows = y_d[l].rearrange("(p n) d -> p n d", n=SLOT_T[l])

                def y_store(e):
                    n = l * N_EXP + e
                    pool.wait_ge(y_act, n + 1)
                    pool.wait_ge(y_dve, n + 1)
                    dma(y_rows[:, e, :], ybuf[e % 2]).then_inc(y_out[e % 2], 16)

                gather(0, xg[0], xg_in[0])
                gather(1, xg[1], xg_in[1])
                if l == 0:
                    modulation_out(ADA_SLOTS)
                else:
                    gates(1, 1)
                for e in range(N_EXP):
                    if e >= 2:
                        pool.wait_ge(xT_mm, 2 * (l * N_EXP + e - 1))
                        gather(e, xg[e % 2], xg_in[e % 2])
                    if e >= 3:
                        y_store(e - 3)
                for e in range(N_EXP - 3, N_EXP):
                    y_store(e)
                for i in range(2):
                    pool.wait_ge(y_out[i], 16 * (l + 1) * N_EXP // 2)

                pool.wait_ge(y_zero, 16 * sum(OV_MAX[:l + 1]))

                def ov_tile(t, _):
                    gather(N_EXP + t, xg[0], ov_xg_in[l])
                    pool.wait_ge(ov_act[l], 4 * t + 4)
                    dma(y_rows[:, N_EXP + t, :], ybuf[0]).then_inc(ov_y_out[l], 16)
                    pool.wait_ge(ov_y_out[l], 16 * (t + 1))
                    pool.nop()

                overflow(pool, l, ov_tile, lambda: pool.nop())
                done = sum(q_tiles(m) for m in range(l))
                for t in range(nq):
                    if t == 2:
                        norm_rows(1, 0, 2)
                    if t >= 2:
                        pool.wait_ge(moe_x, done + t - 1)
                    for k in range(2):
                        pool.indirect_dma_start(yg[t % 2][:, k, :], None, y_d[l],
                                                bass.IndirectOffsetOnAxis(ap=slots[:, t, k:k + 1], axis=0)
                                                ).then_inc(yg_in[t % 2], 16)
                if l == 0:
                    modulation_out(ADA_COMBINE)
                else:
                    dma(R3[:, 0, :], bcast(g["final_g"])).then_inc(fin_in, 16)
            for t in range(LT):
                pool.wait_ge(fin_ready, t + 1)
                dma(out[0, t * P:(t + 1) * P], rowbuf[:, t, :]).then_inc(res_out, 16)
            pool.wait_ge(res_out, 16 * LT)


ROW_LOADS = [5, 10, 15, 18]
N_CONST_LOADS = 3 + 2 * DEPTH

_INS = ["x", "c", "ctx", "c_ctx", "w_ada", "b_ada", "norm1_g", "norm2_g", "w_in", "q_norm_g", "k_norm_g", "na_rpb",
        "ret_decay", "mix_g", "w_out", "w_router", "b_router", "w_exp1", "w_exp3", "w_exp2", "final_g"]


def kernel(**inputs):
    import concourse.bacc as _bacc
    from concourse.bass_utils import run_bass_kernel_spmd as _run

    nc = _bacc.Bacc("TRN2", target_bir_lowering=False, num_devices=1)
    arrays = {f"in_{name}": np.ascontiguousarray(inputs[name]) for name in _INS}
    arrays["in_consts"], arrays["in_ids"], arrays["in_zeros"] = constants()
    g = {n[3:]: nc.dram_tensor(n, a.shape, mybir.dt.from_np(a.dtype), kind="ExternalInput").ap()
         for n, a in arrays.items()}
    out = nc.dram_tensor("out_0", (1, SEQ, D), F32, kind="ExternalOutput").ap()
    trunk(nc, g, out)
    r = _run(nc, [arrays], core_ids=[0])
    return r.results[0]["out_0"]
```

```python
from contextlib import ExitStack

import numpy as np

import concourse.bass as bass
from concourse import mybir

F32 = mybir.dt.float32
F32R = mybir.dt.float32r
I32 = mybir.dt.int32
U32 = mybir.dt.uint32
ALU = mybir.AluOpType
ACT = mybir.ActivationFunctionType
X_AXIS = mybir.AxisListType.X

P = 128
D = 1024
DEPTH = 2
KD = D // P
SEQ = 256
CTX = 256
NT = (SEQ + CTX) // P
LT = SEQ // P
HD = 64
GRID_W = 64
IN_COLS = 2944
N_EXP = 16
F = 512
KF = F // P
EPS = 1e-6
NEG = -1e30
HALF = 512
HPR = 15 * 31
TOP = 8

A_Q, A_K, A_V = 0, 384, 512
N_Q, N_K, N_V = 640, 896, 1152
R_Q, R_K, R_V, R_G = 1408, 1792, 2176, 2560

OV_MAX = [7, 3]
SLOT_T = [N_EXP + n for n in OV_MAX]

RING = 6
WIN_UNITS = 4
N_ADA, N_WIN, N_WOUT, N_MOE = 12, 6, 2, 3 * N_EXP
ADA_START = range(0, 4)
ADA_NORM = range(4, 6)
ADA_RET = range(6, 12)
ADA_MERGE = [range(12, 14), range(21, 22)]
ADA_ROUTE = [range(14, 16), range(22, 23)]
ADA_SLOTS = [range(16, 20), range(23, 24)]
ADA_COMBINE = range(20, 21)
_ada_first = [0] * (DEPTH * N_ADA)
WIN0, WOUT0, MOE0 = [0] * DEPTH, [0] * DEPTH, [0] * DEPTH
STREAM = [("ada", ADA_START), ("ada", ADA_NORM), ("win", 0), ("ada", ADA_RET), ("ada", ADA_MERGE[0]), ("wout", 0),
          ("ada", ADA_ROUTE[0]), ("ada", ADA_SLOTS[0]), ("moe", 0), ("ada", ADA_COMBINE), ("win", 1),
          ("ada", ADA_MERGE[1]), ("wout", 1), ("ada", ADA_ROUTE[1]), ("ada", ADA_SLOTS[1]), ("moe", 1)]
_b = 0
for _kind, _what in STREAM:
    if _kind == "ada":
        for _job in _what:
            _ada_first[_job] = _b
            _b += 1
    else:
        {"win": WIN0, "wout": WOUT0, "moe": MOE0}[_kind][_what] = _b
        _b += {"win": N_WIN + 1, "wout": N_WOUT, "moe": N_MOE}[_kind]
HOLES = [w + N_WIN - 1 for w in WIN0]
assert all(h % RING == RING - 1 for h in HOLES)
ADA_BLOCK = tuple(_ada_first)
N_FIRST = 6
ADA_RUNS = ((6, 14), (14, 21), (21, 22), (22, 24))


def q_tiles(l):
    return NT if l < DEPTH - 1 else LT


def win_block(l, n):
    return WIN0[l] + n + (n == N_WIN - 1)


def win_cols(n):
    return min(HALF, IN_COLS - n * HALF)


def needed(l, t, n):
    width = win_cols(n)
    if t < q_tiles(l):
        return [(0, width)]
    out = []
    for a, b in ((A_K, N_Q), (N_K, R_Q), (R_K, R_G)):
        a, b = max(a - n * HALF, 0), min(b - n * HALF, width)
        if a < b:
            out.append((a, b))
    return [(out[0][0], out[-1][1])] if out else []


PASSES = [(0, (0, 1)), (0, (2, 3))] + [(n, (0, 1, 2, 3)) for n in range(1, N_WIN)]
PROJ = [[(n, t) for n, tiles in PASSES for t in tiles if needed(l, t, n)] for l in range(DEPTH)]
PROJ_BEFORE = [0, len(PROJ[0])]


def proj_bank(n, t):
    return (6, 7, 0, 1)[t] if n % 2 == 0 else 2 + t



ROWS_BEFORE = {}
_n = 0
for _l in range(DEPTH):
    for _what, _count in (("norm1", NT), ("merge", q_tiles(_l)), ("norm2", q_tiles(_l))):
        ROWS_BEFORE[_l, _what] = _n
        _n += _count

PAIRS = {
    "A": [(A_Q + 128 * i, True) for i in range(3)] + [(A_K, False)],
    "N": [(N_Q, True), (N_Q + 128, True), (N_K, False), (N_K + 128, False)],
    "R": [(R_Q + 128 * i, True) for i in range(3)] + [(R_K + 128 * i, False) for i in range(3)],
}
PAIR_SLOT = {"A": 0, "N": 4, "R": 0}
PAIR_FIRST = {"A": 0, "N": 4, "R": 8}
N_PAIRS = 14


def units(l):
    out = []
    for h in range(6):
        for t in range(q_tiles(l)):
            out.append(dict(q=h % 3, base=64 * (h // 3), k=3, v=A_V + 64 * (h // 3), o=A_Q + 64 * h, t=t, bias=None))
    for h in range(4):
        for t in range(q_tiles(l)):
            out.append(dict(q=4 + h // 2, base=64 * (h % 2), k=6 + h // 2, v=N_V + 64 * h, o=N_Q + 64 * h, t=t,
                            bias=h if t < LT else None))
    for u in out:
        u["keys"] = list(range(NT)) if u["t"] < LT else list(range(LT, NT))
    return out


UNITS = [units(l) for l in range(DEPTH)]
UNITS_BEFORE = [0, len(UNITS[0])]
N_RH = 6
MERGED = ((A_Q, 0, 384), (N_Q, 384, 256), (R_Q, 640, 384))


def ret_jobs(l):
    jobs = [((0, 1), 0, "near"), ((2, 3), 0, "far")]
    return jobs + ([((2, 3), 256, "near")] if l < DEPTH - 1 else [])


RJ_BEFORE = [0, N_RH * len(ret_jobs(0))]
RET_BANK = [0, 1, 6]
SCORE_BANK = [0, 1, 6]
LAGS = 384

CONST = {}
_c = 0
for _name, _w in (("ident", 128), ("tri", 128), ("ones", 128), ("lag", 384), ("ahead", 384), ("cos", 128), ("sin", 128),
                  ("mask", 64), ("down", 16), ("up", 16)):
    CONST[_name] = (_c, _w)
    _c += _w
N_CONST = _c


def constants():
    c = np.zeros((P, N_CONST), np.float32)

    def put(name, v):
        a, w = CONST[name]
        c[:, a:a + w] = np.asarray(v, np.float32).reshape(P, w)

    p = np.arange(P)
    put("ident", np.eye(P))
    put("tri", p[:, None] < p[None, :])
    put("ones", np.ones((P, P)))
    lag = np.arange(384)[None, :] - 128 - p[:, None]
    put("lag", lag)
    put("ahead", np.maximum(lag, 0))
    inv = np.float32(10000.0) ** (-np.arange(16, dtype=np.float32) / np.float32(16))
    cos, sin = np.zeros((P, 2, 64)), np.zeros((P, 2, 64))
    for t in range(2):
        tok = t * P + p
        for half, pos in enumerate((tok // GRID_W, tok % GRID_W)):
            ang = (pos.astype(np.float32)[:, None] * inv[None, :]).astype(np.float32).astype(np.float64)
            o = 32 * half
            cos[:, t, o:o + 16] = cos[:, t, o + 16:o + 32] = np.cos(ang)
            sin[:, t, o:o + 16] = -np.sin(ang)
            sin[:, t, o + 16:o + 32] = np.sin(ang)
    put("cos", cos)
    put("sin", sin)
    col = np.arange(GRID_W)
    start = np.clip(col - 8, 0, GRID_W - 16)
    ok = (col[None, :] >= start[:, None]) & (col[None, :] < start[:, None] + 16)
    put("mask", np.where(ok, 0.0, NEG)[p % GRID_W])
    put("down", np.tile(16 - np.arange(16), (P, 1)))
    put("up", np.tile(np.arange(16), (P, 1)))
    ids = np.zeros((P, SLOT_T[0] + NT), np.uint32)
    ids[:, SLOT_T[0]:] = np.arange(NT)[None, :] * P + p[:, None]
    return c, ids, np.zeros((P, D), np.float32)


def trunk(nc, g, out):
    mod_d = nc.dram_tensor("mod_scratch", [DEPTH, 2, 6 * D], F32).ap()
    rpb_d = nc.dram_tensor("rpb_scratch", [DEPTH * 4 * 15, 128], F32).ap()
    near_d = nc.dram_tensor("bias_scratch", [DEPTH * 4 * 15, GRID_W, GRID_W], F32).ap()
    h2_d = [nc.dram_tensor(f"h2_scratch{l}", [q_tiles(l) * P, D], F32).ap() for l in range(DEPTH)]
    slot_d = [nc.dram_tensor(f"slot_token_scratch{l}", [P * SLOT_T[l], 1], U32).ap() for l in range(DEPTH)]
    y_d = [nc.dram_tensor(f"y_scratch{l}", [P * SLOT_T[l], D], F32).ap() for l in range(DEPTH)]

    with ExitStack() as ctx:
        def sb(name, shape, dt=F32):
            return ctx.enter_context(nc.sbuf_tensor("sb_" + name, shape, dt))

        def sem(name):
            return ctx.enter_context(nc.semaphore(name))

        X = sb("x", [P, NT, D])
        with nc.sbuf_tensor("sb_transposed", [P, 8, NT * P], F32) as T:
            pass
        with nc.sbuf_tensor("sb_h_hi", [P, KD, NT * P], F32R) as h_hi:
            pass
        w2_hi = sb("w2_hi", [P, 2, D], F32R)
        w2_lo = sb("w2_lo", [P, 2, D], F32R)
        Z = sb("z", [P, NT * IN_COLS])
        with nc.sbuf_tensor("sb_ring", [P, RING, 4096], F32) as ring:
            pass
        sb("ring_head", [P, RING - 1, 4096])
        win_hi = sb("win_hi", [P, WIN_UNITS, HALF], F32R)
        win_lo = sb("win_lo", [P, WIN_UNITS, HALF], F32R)
        with nc.sbuf_tensor("sb_h_lo", [P, KD, NT * P], F32R) as h_lo:
            pass
        R1 = sb("r1", [P, 2, 1024])
        R3 = sb("r3", [P, 2, 1024])
        with nc.sbuf_tensor("sb_r2", [P, 2, 1024], F32) as R2:
            pass
        actT_hi = sb("actT_hi", [P, 2, KF, P], F32R)
        actT_lo = sb("actT_lo", [P, 2, KF, P], F32R)
        C = sb("constants", [P, N_CONST])
        ids = sb("ids", [P, SLOT_T[0] + NT], U32)
        c_raw = sb("c_raw", [P, 2, KD])
        c_col = sb("c_col", [P, KD, 2])
        w_rt = sb("w_router", [P, KD, N_EXP])
        b_rt = sb("b_router", [P, N_EXP])
        qk_gain = sb("qk_gain", [P, DEPTH, 2, HD])
        lg = sb("log_decay", [P, 4, 2 * DEPTH * N_RH])
        lgt = sb("log_decay_tmp", [P, 2, 2 * DEPTH * N_RH])
        cols = sb("norm_cols", [P, 5, KD])
        eps = sb("eps", [P, 1])
        ss = sb("row_ss", [P, 24])
        rstd = sb("row_rstd", [P, 24])
        hss = sb("head_ss", [P, NT, 16])
        hr = sb("head_rstd", [P, NT, 16])
        soft = sb("soft", [P, 3, 4])
        rw = sb("route_w", [P, NT, 2])
        slots = sb("route_slots", [P, NT, 2], U32)
        ovinfo = sb("overflow_info", [1, TOP], I32)
        slot_tok = sb("slot_tokens", [P, SLOT_T[0]], U32)

        z = Z[:].rearrange("p (t c) -> p t c", t=NT)
        rowbuf = R2
        tables_flat = R1[:].rearrange("p a b -> p (a b)")
        near_tab = [tables_flat[:, 2 * LAGS * i:2 * LAGS * i + LAGS] for i in range(2)]
        far_tab = [tables_flat[:, 2 * LAGS * i + LAGS:2 * LAGS * (i + 1)] for i in range(2)]
        behind = tables_flat[:, 4 * LAGS:5 * LAGS]
        ident = C[:, CONST["ident"][0]:CONST["ident"][0] + 128]

        def const(name):
            a, w = CONST[name]
            return C[:, a:a + w]

        ps = ctx.enter_context(nc.psum_tensor("ps", [P, 8, HALF], F32))

        w_full = [sem(f"w_full{i}") for i in range(RING)]
        w_used = sem("w_used")
        in_c, in_x, in_tables, in_const, in_decay = sem("in_c"), sem("in_x"), sem("in_tables"), sem("in_const"), sem("in_decay")
        in_rpb, rpb_out, bias_spread = sem("in_rpb"), sem("rpb_out"), sem("bias_spread")
        in_brow = [sem(f"in_brow{i}") for i in range(2)]
        mod_out = [sem(f"mod_out{i}") for i in range(2)]
        in_brow_first, mod_out_first = sem("in_brow_first"), sem("mod_out_first")
        in_cols, cols_ready = sem("in_cols"), sem("cols_ready")
        in_rows, in_mix, in_gate, in_bias = sem("in_rows"), sem("in_mix"), sem("in_gate"), sem("in_bias")
        h2_out = [sem(f"h2_out{i}") for i in range(2)]
        y_zero, slot_zero, slot_out, slot_in = sem("y_zero"), sem("slot_zero"), sem("slot_out"), sem("slot_in")
        xg_in = [sem(f"xg_in{i}") for i in range(2)]
        y_out = [sem(f"y_out{i}") for i in range(2)]
        yg_in = [sem(f"yg_in{i}") for i in range(NT)]
        ov_w_in = [sem(f"ov_w_in{l}") for l in range(DEPTH)]
        ov_xg_in = [sem(f"ov_xg_in{l}") for l in range(DEPTH)]
        ov_y_out = [sem(f"ov_y_out{l}") for l in range(DEPTH)]
        fin_in, res_out = sem("fin_in"), sem("res_out")
        dve_step, act_step = sem("dve_step"), sem("act_step")
        pad_zero, eps_set = sem("pad_zero"), sem("eps_set")
        silu_c, decay_u, decay_ready = sem("silu_c"), sem("decay_u"), sem("decay_ready")
        ada_mm, ada_ev = sem("ada_mm"), sem("ada_ev")
        row_sq, row_std, row_ready = sem("row_sq"), sem("row_std"), sem("row_ready")
        rowT_mm, rowT_act, rowT_dve = sem("rowT_mm"), sem("rowT_act"), sem("rowT_dve")
        h_round, h_split = sem("h_round"), sem("h_split")
        win_rounded, win_split, win_free = sem("win_rounded"), sem("win_split"), sem("win_free")
        proj_mm, proj_act, proj_dve = sem("proj_mm"), sem("proj_act"), sem("proj_dve")
        qk_ss, qk_std, qk_ready = sem("qk_ss"), sem("qk_std"), sem("qk_ready")
        bias_ready, na_done = sem("bias_ready"), sem("na_done")
        pair_mm, pair_act, pair_dve = sem("pair_mm"), sem("pair_act"), sem("pair_dve")
        score_mm, max_ready, probs_ready = sem("score_mm"), sem("max_ready"), sem("probs_ready")
        pT_mm, pT_ev, o_mm, o_ev = sem("pT_mm"), sem("pT_ev"), sem("o_mm"), sem("o_ev")
        behind_ready, decay_exp, w_ready = sem("behind_ready"), sem("decay_exp"), sem("w_ready")
        rscore_mm, rscore_w, ro_mm, ro_ev = sem("rscore_mm"), sem("rscore_w"), sem("ro_mm"), sem("ro_ev")
        mg_sq, mg_ss, mg_std, silu_g = sem("mg_sq"), sem("mg_ss"), sem("mg_std"), sem("silu_g")
        wout_mm, x_upd = sem("wout_mm"), sem("x_upd")
        rt_mm, rt_max, rt_exp, rt_sel, rank_mm = sem("rt_mm"), sem("rt_max"), sem("rt_exp"), sem("rt_sel"), sem("rank_mm")
        slots_ready = sem("slots_ready")
        xT_mm, xT_act, xT_dve = sem("xT_mm"), sem("xT_act"), sem("xT_dve")
        silu_h, act_ready = sem("silu_h"), sem("act_ready")
        w2_rounded, w2_split, w2_free, aT_hi = sem("w2_rounded"), sem("w2_split"), sem("w2_free"), sem("aT_hi")
        aT_mm, aT_ev, y_mm, y_act, y_dve = sem("aT_mm"), sem("aT_ev"), sem("y_mm"), sem("y_act"), sem("y_dve")
        ov_pe = [sem(f"ov_pe{l}") for l in range(DEPTH)]
        ov_act = [sem(f"ov_act{l}") for l in range(DEPTH)]
        ov_dve = [sem(f"ov_dve{l}") for l in range(DEPTH)]
        comb_mul, moe_x, fin_ready = sem("comb_mul"), sem("moe_x"), sem("fin_ready")

        def full(b):
            skipped = sum(h < b and h % RING == b % RING for h in HOLES)
            return w_full[b % RING], 16 * (b // RING + 1 - skipped)

        rpb_pad = Z[0:120, 4096:4096 + P]

        def modrow(job):
            if job < N_FIRST:
                return Z[0:2, job * HALF:(job + 1) * HALF]
            return R3[0:2, 1, (job % 2) * HALF:(job % 2 + 1) * HALF]

        def row_uses(job):
            return (job - N_FIRST) // 2 + 1

        def moe_block(l, e, m):
            if m == 2:
                return MOE0[l] + 3 * e + (3 if e < N_EXP - 1 else 2)
            return MOE0[l] + (m if e == 0 else 3 * e - 1 + 2 * m)

        xg = [Z[:, 1024 * i:1024 * (i + 1)] for i in range(2)]
        xgT = [Z[:, 2048 + 1024 * i:3072 + 1024 * i].rearrange("p (k t) -> p k t", k=KD) for i in range(2)]
        s1 = Z[:, 4096:4608]
        act_sb = Z[:, 4608:5120]
        ov_actT = Z[:, 5120:5632].rearrange("p (k t) -> p k t", k=KF)
        ybuf = [Z[:, 6144 + 1024 * i:7168 + 1024 * i] for i in range(2)]
        yg = [Z[:, 2048 * i:2048 * (i + 1)].rearrange("p (k c) -> p k c", k=2) for i in range(NT)]
        moe_gate = [Z[:, NT * IN_COLS - D * (2 - s):NT * IN_COLS - D * (1 - s)] for s in range(2)]
        rtmp = Z[:, 8192:8192 + 30 * 64 + 64]
        rows = [Z[:, 1024 * i:1024 * (i + 1)] for i in range(5)]

        def overflow(eng, l, tile, ready):
            eng.wait_ge(slots_ready, l + 1)
            n_ov = eng.value_load(ovinfo[0:1, 0:1], min_val=0, max_val=OV_MAX[0])
            with eng.If(n_ov > 0):
                ready()
                tile(0, n_ov)
                for t in range(1, OV_MAX[l]):
                    with eng.If(n_ov > t):
                        tile(t, n_ov)
                    eng.nop()
            eng.nop()

        block = ctx.enter_context(nc.Block())

        @block.sync
        def _(sp):
            def load(b, dst, src):
                if b >= RING:
                    sp.wait_ge(w_used, b - RING + 1)
                sp.dma_start(dst, src).then_inc(full(b)[0], 16)

            def slot(b):
                return ring[:, b % RING, :]

            def ada(jobs):
                for job in jobs:
                    b, l, n = ADA_BLOCK[job], job // N_ADA, job % N_ADA
                    load(b, slot(b).rearrange("p (k c) -> p k c", k=KD),
                         g["w_ada"][l].rearrange("(p k) c -> p k c", k=KD)[:, :, n * HALF:(n + 1) * HALF])

            def w13(w, l, e):
                return w[l, e].rearrange("(p k) f -> p (k f)", k=KD)

            def w2(l, e):
                return g["w_exp2"][l, e].rearrange("(p k) c -> p (k c)", k=KF)

            sp.dma_start(c_raw[:, 0, :], g["c"].rearrange("o (p k) -> p (o k)", k=KD)).then_inc(in_c, 16)
            sp.dma_start(c_raw[:, 1, :], g["c_ctx"].rearrange("(p k) -> p k", k=KD)).then_inc(in_c, 16)
            ada(ADA_START)
            ada(ADA_NORM)
            for l in range(DEPTH):
                for n in range(N_WIN):
                    if l == 0 and n == 0:
                        sp.wait_ge(in_cols, 16 * 5)
                    if l and n == 1:
                        sp.wait_ge(yg_in[NT - 1], 32)
                    b, c = win_block(l, n), win_cols(n)
                    load(b, slot(b)[:, 0:KD * c].rearrange("p (k c) -> p k c", k=KD),
                         g["w_in"][l].rearrange("(p k) c -> p k c", k=KD)[:, :, n * HALF:n * HALF + c])
                if l == 0:
                    ada(ADA_RET)
                ada(ADA_MERGE[l])
                for n in range(N_WOUT):
                    b = WOUT0[l] + n
                    load(b, slot(b).rearrange("p (k c) -> p k c", k=KD),
                         g["w_out"][l].rearrange("(p k) c -> p k c", k=KD)[:, :, n * HALF:(n + 1) * HALF])
                ada(ADA_ROUTE[l])
                ada(ADA_SLOTS[l])
                load(moe_block(l, 0, 0), slot(moe_block(l, 0, 0)), w13(g["w_exp1"], l, 0))
                load(moe_block(l, 0, 1), slot(moe_block(l, 0, 1)), w13(g["w_exp3"], l, 0))

                def turn(e, b0, off):
                    for m, src in enumerate((w13(g["w_exp1"], l, e), w2(l, e - 1), w13(g["w_exp3"], l, e))):
                        b = b0 + m
                        sp.wait_ge(w_used, off + b - RING + 1)
                        sp.dma_start(slot(b), src).then_inc(full(b)[0], 16)

                turn(1, moe_block(l, 1, 0), 0)
                turn(2, moe_block(l, 2, 0), 0)
                with sp.Fori(0, (N_EXP - 4) // 2) as i:
                    for e in (3, 4):
                        turn(i * 2 + e, moe_block(l, e, 0), i * RING)
                turn(N_EXP - 1, moe_block(l, N_EXP - 1, 0), 0)
                b = moe_block(l, N_EXP - 1, 2)
                load(b, slot(b), w2(l, N_EXP - 1))

                def ov_tile(t, n_ov):
                    eid = sp.value_load(ovinfo[0:1, 1 + t:2 + t], min_val=0, max_val=N_EXP - 1)
                    for m, src in enumerate((w13(g["w_exp1"], l, eid), w13(g["w_exp3"], l, eid), w2(l, eid))):
                        sp.dma_start(ring[:, m, :], src).then_inc(ov_w_in[l], 16)
                    sp.wait_ge(ov_pe[l], 4 * t + 4)
                    sp.nop()

                overflow(sp, l, ov_tile, lambda: sp.wait_ge(w_used, MOE0[l] + N_MOE))
                if l == 0:
                    ada(ADA_COMBINE)

        @block.tensor
        def _(pe):
            mm, tp = nc.tensor.matmul, nc.tensor.transpose

            def ada(jobs, bank0=0):
                for job in jobs:
                    b = ADA_BLOCK[job]
                    if job >= 2:
                        pe.wait_ge(ada_ev, job - 1)
                    pe.wait_ge(*full(b))
                    w = ring[:, b % RING, :].rearrange("p (k c) -> p k c", k=KD)
                    for k in range(KD):
                        last = mm(ps[0:2, bank0 + job % 2, :], c_col[:, k, :], w[:, k, :], start=(k == 0), stop=(k == KD - 1))
                    last.then_inc(w_used, 1)

            def rows_transposed(n):
                pe.wait_ge(row_ready, n + 1)
                if n >= 2:
                    pe.wait_ge(rowT_act, n - 1)
                    pe.wait_ge(rowT_dve, n - 1)
                src = rowbuf[:, n % 2, :].rearrange("p (c k) -> p k c", k=KD)
                for half in range(2):
                    for q in range(4):
                        last = tp(ps[:, 2 + 2 * (n % 2) + half, q * P:(q + 1) * P], src[:, 4 * half + q, :], ident)
                    last.then_inc(rowT_mm, 1)

            def projection(l):
                first = ROWS_BEFORE[l, "norm1"]
                rows_transposed(first)
                rows_transposed(first + 1)
                pe.wait_ge(ada_ev, (ADA_COMBINE if l else ADA_NORM)[-1] + 1)
                job = PROJ_BEFORE[l]
                for i, (n, tiles) in enumerate(PASSES):
                    tiles = [t for t in tiles if needed(l, t, n)]
                    pe.wait_ge(h_split, NT * l + tiles[-1] + 1)
                    if n >= 2:
                        before = PROJ_BEFORE[l] + sum(m < n - 1 for m, _ in PROJ[l])
                        pe.wait_ge(proj_act, (before + 1) // 2)
                        pe.wait_ge(proj_dve, before // 2)
                    for k in range(KD):
                        if i == 0 and k == KD // 2:
                            rows_transposed(first + 2)
                            rows_transposed(first + 3)
                        u = (len(PASSES) * l + i) * KD + k
                        pe.wait_ge(win_split, u + 1)
                        w_hi, w_lo = win_hi[:, u % WIN_UNITS, :], win_lo[:, u % WIN_UNITS, :]
                        for t in tiles:
                            x_hi, x_lo = h_hi[:, k, t * P:(t + 1) * P], h_lo[:, k, t * P:(t + 1) * P]
                            for lo, hi in needed(l, t, n):
                                o = ps[:, proj_bank(n, t), lo:hi]
                                mm(o, x_hi, w_hi[:, lo:hi], start=(k == 0), stop=False)
                                mm(o, x_hi, w_lo[:, lo:hi], start=False, stop=False)
                                last = mm(o, x_lo, w_hi[:, lo:hi], start=False, stop=(k == KD - 1))
                            if k == KD - 1:
                                last.then_inc(proj_mm, 1)
                                job += 1
                        if k < KD - 1:
                            last.then_inc(win_free, 1)
                    if i:
                        pe.wait_ge(proj_mm, job)
                        pe.sem_inc(w_used, 2 if n == N_WIN - 1 else 1)

            def pairs(l, group):
                for i, (c0, is_q) in enumerate(PAIRS[group]):
                    job = l * N_PAIRS + PAIR_FIRST[group] + i
                    if job >= 4:
                        pe.wait_ge(pair_act if job % 2 == 0 else pair_dve, (job - 4) // 2 + 1)
                    for t in range(q_tiles(l) if is_q else NT):
                        last = tp(ps[:, 2 + job % 4, t * P:(t + 1) * P], z[:, t, c0:c0 + P], ident)
                    last.then_inc(pair_mm, 1)

            def pairs_moved(l, group):
                n = (l * N_PAIRS + PAIR_FIRST[group] + len(PAIRS[group])) // 2
                pe.wait_ge(pair_act, n)
                pe.wait_ge(pair_dve, n)

            def attention(l):
                us, before = UNITS[l], UNITS_BEFORE[l]

                def scores(i):
                    u, n = us[i], before + i
                    if n >= 3:
                        pe.wait_ge(probs_ready, n - 2)
                    bank = ps[:, SCORE_BANK[n % 3], :]
                    q = T[u["base"]:u["base"] + HD, u["q"], u["t"] * P:(u["t"] + 1) * P]
                    k = T[u["base"]:u["base"] + HD, u["k"], :]
                    if u["bias"] is None:
                        last = mm(bank[:, 0:P * len(u["keys"])], q, k[:, P * u["keys"][0]:], start=True, stop=True)
                    else:
                        pe.wait_ge(bias_ready, l + 1)
                        bias = R3[:].rearrange("p a b -> p (a b)").rearrange("p (h t k) -> p h t k", h=4, t=2)
                        mm(bank[:, 0:SEQ], q, k[:, 0:SEQ], start=True, stop=False)
                        mm(bank[:, 0:SEQ], ident, bias[:, u["bias"], u["t"], :], start=False, stop=True)
                        last = mm(bank[:, SEQ:], q, k[:, SEQ:], start=True, stop=True)
                    last.then_inc(score_mm, 1)

                def probs_transposed(i):
                    u, n = us[i], before + i
                    pe.wait_ge(probs_ready, n + 1)
                    if n >= 2:
                        pe.wait_ge(pT_ev, n - 1)
                    for c in range(len(u["keys"])):
                        last = tp(ps[:, 2 + n % 2, c * P:(c + 1) * P],
                                  R2[:, 0, (n % 2) * HALF + c * P:(n % 2) * HALF + (c + 1) * P], ident)
                    last.then_inc(pT_mm, 1)

                def output(i):
                    u, n = us[i], before + i
                    pe.wait_ge(pT_ev, n + 1)
                    if n >= 2:
                        pe.wait_ge(o_ev, n - 1)
                    for c, kt in enumerate(u["keys"]):
                        last = mm(ps[:, 4 + n % 2, 0:HD], R2[:, 1, (n % 2) * HALF + c * P:(n % 2) * HALF + (c + 1) * P],
                                  z[:, kt, u["v"]:u["v"] + HD], start=(c == 0), stop=(c == len(u["keys"]) - 1))
                    last.then_inc(o_mm, 1)

                scores(0)
                scores(1)
                for i in range(len(us) + 1):
                    if i + 2 < len(us):
                        scores(i + 2)
                    if i < len(us):
                        probs_transposed(i)
                    if i >= 1:
                        output(i - 1)

            def retention(l):
                jobs, nj = ret_jobs(l), len(ret_jobs(l))

                def scores(r):
                    base, pair = HD * (r % 2), r // 2
                    for j, (keys, q0, _) in enumerate(jobs):
                        job = RJ_BEFORE[l] + r * nj + j
                        if r:
                            pe.wait_ge(rscore_w, job - nj + 1)
                        for kk, kt in enumerate(keys):
                            last = mm(ps[:, RET_BANK[j], (1 - kk) * 256:(2 - kk) * 256],
                                      T[base:base + HD, 3 + pair, kt * P:(kt + 1) * P],
                                      T[base:base + HD, pair, q0:q0 + 256], start=True, stop=True)
                        last.then_inc(rscore_mm, 1)

                def output(r):
                    head = l * N_RH + r
                    pe.wait_ge(rscore_w, RJ_BEFORE[l] + (r + 1) * nj)
                    if head >= 2:
                        pe.wait_ge(ro_ev, head - 1)
                    for t in range(q_tiles(l)):
                        use = (0, 1) if t < LT else (2,)
                        parts = [(j, kk, kt) for j in use for kk, kt in enumerate(jobs[j][0])]
                        for x, (j, kk, kt) in enumerate(parts):
                            job = RJ_BEFORE[l] + r * nj + j
                            at = (1 - kk) * 256 + (t % LT) * P
                            w = R2[:, (job % 4) // 2, (job % 2) * HALF + at:(job % 2) * HALF + at + P]
                            last = mm(ps[:, 7 - 2 * (head % 2), t * HD:(t + 1) * HD], w,
                                      z[:, kt, R_V + HD * r:R_V + HD * (r + 1)],
                                      start=(x == 0), stop=(x == len(parts) - 1))
                    last.then_inc(ro_mm, 1)

                scores(0)
                for r in range(N_RH):
                    if l == 0:
                        ada([ADA_RET[r]], 2)
                    if r + 1 < N_RH:
                        scores(r + 1)
                    output(r)

            def out_projection(l, t):
                n = ROWS_BEFORE[l, "merge"] + t
                pe.wait_ge(rowT_act, n + 1)
                pe.wait_ge(rowT_dve, n + 1)
                for half in range(2):
                    job, b = 2 * (NT * l + t) + half, WOUT0[l] + half
                    if job >= 2:
                        pe.wait_ge(x_upd, job - 1)
                    pe.wait_ge(*full(b))
                    w = ring[:, b % RING, :].rearrange("p (k c) -> p k c", k=KD)
                    for k in range(KD):
                        last = mm(ps[:, 6 + half, :], T[:, k, t * P:(t + 1) * P], w[:, k, :],
                                  start=(k == 0), stop=(k == KD - 1))
                    last.then_inc(wout_mm, 1)

            def router(l):
                n = ROWS_BEFORE[l, "norm2"] + q_tiles(l)
                pe.wait_ge(rowT_act, n)
                pe.wait_ge(rowT_dve, n)
                pe.wait_ge(x_upd, 2 * (NT * l + q_tiles(l)))
                for t in range(q_tiles(l)):
                    for k in range(KD):
                        last = mm(ps[:, 6, t * N_EXP:(t + 1) * N_EXP], T[:, k, t * P:(t + 1) * P], w_rt[:, k, :],
                                  start=(k == 0), stop=(k == KD - 1))
                last.then_inc(rt_mm, 1)

            def ranks(l):
                nq = q_tiles(l)
                pe.wait_ge(rt_sel, l + 1)
                sel = rtmp[:, 0:nq * N_EXP]
                for t in range(nq + 1):
                    for s in range(min(t + 1, nq)):
                        last = mm(ps[:, 7, t * N_EXP:(t + 1) * N_EXP], const("tri" if s == t else "ones"),
                                  sel[:, s * N_EXP:(s + 1) * N_EXP], start=(s == 0), stop=(s == min(t, nq - 1)))
                last.then_inc(rank_mm, 1)

            def x_transposed(src):
                v = src.rearrange("p (c k) -> p k c", k=KD)
                for half in range(2):
                    for q in range(4):
                        last = tp(ps[:, 4 + half, q * P:(q + 1) * P], v[:, 4 * half + q, :], ident)
                    last.then_inc(xT_mm, 1)

            def moe(l):
                def xT(e, i):
                    n = l * N_EXP + e
                    pe.wait_ge(xg_in[e % 2], i * 16 + 16 * (n // 2 + 1))
                    if n:
                        pe.wait_ge(xT_act, i * 2 + n)
                        pe.wait_ge(xT_dve, i * 2 + n)
                    x_transposed(xg[e % 2])

                def h(e, i, m):
                    n, b = l * N_EXP + e, moe_block(l, e, m)
                    if m == 0:
                        pe.wait_ge(xT_act, i * 2 + (n + 1))
                        pe.wait_ge(xT_dve, i * 2 + (n + 1))
                    if n:
                        pe.wait_ge(silu_h if m == 0 else act_ready, i * 2 + n)
                    pe.wait_ge(full(b)[0], i * 16 + full(b)[1])
                    for k in range(KD):
                        last = mm(ps[:, m, :], xgT[e % 2][:, k, :], ring[:, b % RING, k * F:(k + 1) * F],
                                  start=(k == 0), stop=(k == KD - 1))
                    last.then_inc(w_used, 1)

                def aT(e, i):
                    n = l * N_EXP + e
                    pe.wait_ge(act_ready, i * 2 + (n + 1))
                    if n:
                        pe.wait_ge(aT_ev, i * 2 + n)
                    v = act_sb.rearrange("p (c k) -> p k c", k=KF)
                    for k in range(KF):
                        last = tp(ps[:, 6, k * P:(k + 1) * P], v[:, k, :], ident)
                    last.then_inc(aT_mm, 1)

                def y(e, i):
                    n, b = l * N_EXP + e, moe_block(l, e, 2)
                    pe.wait_ge(aT_ev, i * 2 + (n + 1))
                    if n:
                        pe.wait_ge(y_act, i * 2 + n)
                        pe.wait_ge(y_dve, i * 2 + n)
                    for k in range(KF):
                        for half in range(2):
                            pe.wait_ge(w2_split, i * 4 * KF + (2 * KF * n + 2 * k + half + 1))
                            cols = slice(half * HALF, (half + 1) * HALF)
                            a_hi, a_lo = actT_hi[:, e % 2, k, :], actT_lo[:, e % 2, k, :]
                            w_hi, w_lo = w2_hi[:, k % 2, cols], w2_lo[:, k % 2, cols]
                            mm(ps[:, 2 + half, :], a_hi, w_hi, start=(k == 0), stop=False)
                            mm(ps[:, 2 + half, :], a_hi, w_lo, start=False, stop=False)
                            last = mm(ps[:, 2 + half, :], a_lo, w_hi, start=False, stop=(k == KF - 1))
                            if k == KF - 1:
                                last.then_inc(y_mm if half == 0 else w_used, 1)
                            else:
                                last.then_inc(w2_free, 1)

                def turn(e, i, more=True):
                    h(e, i, 0)
                    y(e - 1, i)
                    h(e, i, 1)
                    if more:
                        xT(e + 1, i)
                    aT(e, i)

                xT(0, 0)
                h(0, 0, 0)
                h(0, 0, 1)
                xT(1, 0)
                aT(0, 0)
                turn(1, 0)
                turn(2, 0)
                with pe.Fori(0, (N_EXP - 4) // 2) as i:
                    turn(3, i)
                    turn(4, i)
                turn(N_EXP - 1, 0, more=False)
                y(N_EXP - 1, 0)

            def ov_tile(l):
                def tile(t, _):
                    pe.wait_ge(ov_xg_in[l], 16 * (t + 1))
                    v = xg[0].rearrange("p (c k) -> p k c", k=KD)
                    for k in range(KD):
                        last = tp(ps[:, 4 + k // 4, (k % 4) * P:(k % 4 + 1) * P], v[:, k, :], ident)
                    last.then_inc(ov_pe[l], 1)
                    pe.wait_ge(ov_act[l], 4 * t + 1)
                    pe.wait_ge(ov_w_in[l], 48 * (t + 1))
                    for m in range(2):
                        for k in range(KD):
                            last = mm(ps[:, m, :], xgT[0][:, k, :], ring[:, m, k * F:(k + 1) * F],
                                      start=(k == 0), stop=(k == KD - 1))
                    last.then_inc(ov_pe[l], 1)
                    pe.wait_ge(ov_dve[l], t + 1)
                    v = act_sb.rearrange("p (c k) -> p k c", k=KF)
                    for k in range(KF):
                        last = tp(ps[:, 6, k * P:(k + 1) * P], v[:, k, :], ident)
                    last.then_inc(ov_pe[l], 1)
                    pe.wait_ge(ov_act[l], 4 * t + 3)
                    for half in range(2):
                        for k in range(KF):
                            last = mm(ps[:, 2 + half, :], ov_actT[:, k, :],
                                      ring[:, 2, k * D + half * HALF:k * D + (half + 1) * HALF],
                                      start=(k == 0), stop=(k == KF - 1))
                    last.then_inc(ov_pe[l], 1)
                return tile

            def ov_ready(l):
                pe.wait_ge(y_act, (l + 1) * N_EXP)
                pe.wait_ge(y_dve, (l + 1) * N_EXP)

            pe.wait_ge(silu_c, 1)
            ada(ADA_START)
            ada(ADA_NORM)
            pe.wait_ge(in_tables, 16)
            for l in range(DEPTH):
                nq = q_tiles(l)
                if l:
                    ada(ADA_COMBINE)
                projection(l)
                n = PROJ_BEFORE[l] + len(PROJ[l])
                pe.wait_ge(proj_act, (n + 1) // 2)
                pe.wait_ge(proj_dve, n // 2)
                pe.wait_ge(qk_ready, NT * (l + 1))
                pairs(l, "A")
                pairs(l, "N")
                pairs_moved(l, "A")
                pairs_moved(l, "N")
                attention(l)
                pe.wait_ge(o_ev, UNITS_BEFORE[l] + len(UNITS[l]))
                pairs(l, "R")
                pairs_moved(l, "R")
                retention(l)
                ada(ADA_MERGE[l])
                if l == 0:
                    pe.wait_ge(ada_ev, ADA_RET[-1] + 1)
                for t in range(2):
                    rows_transposed(ROWS_BEFORE[l, "merge"] + t)
                for t in range(nq):
                    out_projection(l, t)
                    if t + 2 < nq:
                        rows_transposed(ROWS_BEFORE[l, "merge"] + t + 2)
                    if nq > 2 and t == 2:
                        rows_transposed(ROWS_BEFORE[l, "norm2"])
                pe.wait_ge(wout_mm, 2 * (NT * l + nq))
                pe.sem_inc(w_used, N_WOUT)
                for t in range(1 if nq > 2 else 0, nq):
                    rows_transposed(ROWS_BEFORE[l, "norm2"] + t)
                router(l)
                ada(ADA_ROUTE[l])
                ranks(l)
                ada(ADA_SLOTS[l])
                pe.wait_ge(ada_ev, ADA_SLOTS[l][-1] + 1)
                moe(l)
                overflow(pe, l, ov_tile(l), lambda: ov_ready(l))

        norm_tiles = {}
        for l in range(DEPTH):
            for what in ("norm1", "norm2"):
                norm_tiles[l, what] = len(norm_tiles)
        NORMS_BEFORE = {(0, "norm1"): 0, (0, "norm2"): NT, (1, "norm1"): NT + q_tiles(0),
                        (1, "norm2"): 2 * NT + q_tiles(0), "final": 2 * NT + q_tiles(0) + q_tiles(1)}

        def h2_stored(n, parity):
            return 16 * sum(m % 2 == parity for l in range(DEPTH)
                            for m in range(ROWS_BEFORE[l, "norm2"], ROWS_BEFORE[l, "norm2"] + q_tiles(l)) if m < n)

        @block.scalar
        def _(act):
            A = nc.scalar.activation
            step = [0]

            def square_sqrt(x, dst, k):
                A(dst, x, ACT.Square, accum_out=ss[:, k:k + 1]).then_inc(row_sq, 1)
                act.wait_ge(row_sq, k + 1)
                A(rstd[:, k:k + 1], ss[:, k:k + 1], ACT.Sqrt, bias=eps[:], scale=1.0 / D).then_inc(row_std, 1)

            def norm_stat(l, what, t):
                n, k = ROWS_BEFORE[l, what] + t, NORMS_BEFORE[l, what] + t
                if what == "norm2":
                    act.wait_ge(x_upd, 2 * (NT * l + t + 1))
                elif l:
                    act.wait_ge(moe_x, sum(q_tiles(m) for m in range(l - 1)) + t + 1)
                if n >= 2:
                    act.wait_ge(rowT_mm, 2 * (n - 1))
                if what == "norm1" and t >= 2:
                    act.wait_ge(h_split, NT * l + t - 1)
                if h2_stored(n, n % 2):
                    act.wait_ge(h2_out[n % 2], h2_stored(n, n % 2))
                square_sqrt(X[:, t, :], rowbuf[:, n % 2, :], k)

            def rows_moved(n, t):
                act.wait_ge(rowT_mm, 2 * n + 1)
                A(T[:, 0:4, t * P:(t + 1) * P], ps[:, 2 + 2 * (n % 2), :].rearrange("p (k c) -> p k c", k=4),
                  ACT.Copy).then_inc(rowT_act, 1)

            def cols_moved(l, t):
                n, s = ROWS_BEFORE[l, "norm1"] + t, 2 * (t // LT)
                act.wait_ge(cols_ready, l + 1)
                act.wait_ge(rowT_mm, 2 * n + 2)
                row = rowbuf[:, n % 2, :].rearrange("p (k c) -> p k c", k=KD)
                for k in range(4):
                    last = A(row[:, k, :], ps[:, 2 + 2 * (n % 2), k * P:(k + 1) * P], ACT.Identity,
                             bias=cols[:, s + 1, k:k + 1], scale=cols[:, s, k:k + 1])
                last.then_inc(rowT_act, 1)
                act.wait_ge(rowT_act, n + 1)
                act.wait_ge(rowT_dve, n + 1)
                A(h_hi[:, :, t * P:(t + 1) * P], row, ACT.Copy).then_inc(h_round, 1)

            def win_rounds(l, i, chunks=range(KD)):
                n = PASSES[i][0]
                b, c = win_block(l, n), win_cols(n)
                act.wait_ge(*full(b))
                for k in chunks:
                    u = (len(PASSES) * l + i) * KD + k
                    p, kk = (u - WIN_UNITS) // KD, (u - WIN_UNITS) % KD
                    if p >= len(PASSES) * l:
                        if kk < KD - 1:
                            act.wait_ge(win_free, p * (KD - 1) + kk + 1)
                        else:
                            done = sum(len([t for t in tiles if needed(l, t, m)])
                                       for m, tiles in PASSES[:p - len(PASSES) * l + 1])
                            act.wait_ge(proj_mm, PROJ_BEFORE[l] + done)
                    A(win_hi[:, u % WIN_UNITS, 0:c], ring[:, b % RING, k * c:(k + 1) * c], ACT.Copy).then_inc(win_rounded, 1)

            def norm(l, what, count):
                n = ROWS_BEFORE[l, what]
                for t in range(count):
                    rows_moved(n + t, t)
                    if t + 2 < count:
                        norm_stat(l, what, t + 2)

            def attention(l):
                us, before = UNITS[l], UNITS_BEFORE[l]

                def exponentials(i):
                    n, cols = before + i, P * len(us[i]["keys"])
                    act.wait_ge(max_ready, n + 1)
                    if n >= 2:
                        act.wait_ge(pT_mm, n - 1)
                    if n >= 4:
                        act.wait_ge(o_ev, n - 3)
                    A(R2[:, 0, (n % 2) * HALF:(n % 2) * HALF + cols], ps[:, SCORE_BANK[n % 3], 0:cols], ACT.Exp,
                      bias=soft[:, 0, n % 4:n % 4 + 1], accum_out=soft[:, 1, n % 4:n % 4 + 1]).then_inc(probs_ready, 1)

                def transposed_moved(i):
                    n, cols = before + i, P * len(us[i]["keys"])
                    act.wait_ge(pT_mm, n + 1)
                    if n >= 2:
                        act.wait_ge(o_mm, n - 1)
                    A(R2[:, 1, (n % 2) * HALF:(n % 2) * HALF + cols], ps[:, 2 + n % 2, 0:cols],
                      ACT.Copy).then_inc(pT_ev, 1)

                exponentials(0)
                for i in range(len(us)):
                    if i + 1 < len(us):
                        exponentials(i + 1)
                    transposed_moved(i)

            def retention(l):
                lag, ahead = const("lag"), const("ahead")

                def decays(r):
                    head = l * N_RH + r
                    f, b = 2 * N_RH * l + r, 2 * N_RH * l + N_RH + r
                    near, far = near_tab[r % 2], far_tab[r % 2]
                    if r >= 2:
                        act.wait_ge(rscore_w, RJ_BEFORE[l] + (r - 1) * len(ret_jobs(l)))
                    A(near, ahead, ACT.Exp, scale=lg[:, 0, f:f + 1]).then_inc(decay_exp, 1)
                    A(far, lag, ACT.Exp, bias=lg[:, 2, f:f + 1], scale=lg[:, 0, f:f + 1]).then_inc(decay_exp, 1)
                    if r:
                        act.wait_ge(w_ready, head)
                    A(T[:, 6, 0:LAGS], behind, ACT.Exp, scale=lg[:, 1, b:b + 1]).then_inc(decay_exp, 1)
                    A(T[:, 7, 0:LAGS], lag, ACT.Exp, bias=lg[:, 2, b:b + 1], scale=lg[:, 1, b:b + 1]).then_inc(decay_exp, 1)

                def moved(r):
                    head, nq = l * N_RH + r, q_tiles(l)
                    act.wait_ge(ro_mm, head + 1)
                    A(z[:, 0:nq, R_Q + HD * r:R_Q + HD * (r + 1)],
                      ps[:, 7 - 2 * (head % 2), 0:nq * HD].rearrange("p (t d) -> p t d", d=HD),
                      ACT.Copy).then_inc(ro_ev, 1)

                act.wait_ge(behind_ready, l + 1)
                decays(0)
                decays(1)
                for r in range(N_RH):
                    if r + 2 < N_RH:
                        decays(r + 2)
                    if r == 0:
                        for t in range(q_tiles(l)):
                            last = A(z[:, t, R_G:], z[:, t, R_G:], ACT.Silu)
                        last.then_inc(silu_g, 1)
                    moved(r)

            def moe(l):
                def xT_moved(e, i):
                    n = l * N_EXP + e
                    act.wait_ge(xT_mm, i * 4 + (2 * n + 1))
                    A(xgT[e % 2][:, 0:4, :], ps[:, 4, :].rearrange("p (k c) -> p k c", k=4),
                      ACT.Copy).then_inc(xT_act, 1)

                def silu(e, i):
                    n = l * N_EXP + e
                    act.wait_ge(w_used, i * RING + (moe_block(l, e, 0) + 1))
                    if n:
                        act.wait_ge(act_ready, i * 2 + n)
                    A(s1, ps[:, 0, :], ACT.Silu).then_inc(silu_h, 1)

                def aT_moved(e, i):
                    n = l * N_EXP + e
                    act.wait_ge(aT_mm, i * 2 + (n + 1))
                    A(actT_hi[:, e % 2, :, :].rearrange("p k c -> p (k c)"), ps[:, 6, :], ACT.Copy).then_inc(aT_hi, 1)

                def w2_rounds(e, i):
                    n, b = l * N_EXP + e, moe_block(l, e, 2)
                    act.wait_ge(full(b)[0], i * 16 + full(b)[1])
                    for u in range(2 * KF):
                        if u >= 4:
                            act.wait_ge(w2_free, i * 12 + (6 * n + u - 3))
                        elif n and u < 2:
                            act.wait_ge(w2_free, i * 12 + (6 * n + u - 1))
                        elif n and u == 2:
                            act.wait_ge(y_mm, i * 2 + n)
                        elif n:
                            act.wait_ge(w_used, i * RING + (moe_block(l, e - 1, 2) + 1 if e else MOE0[l]))
                        A(w2_hi[:, u % 4 // 2, u % 2 * HALF:(u % 2 + 1) * HALF],
                          ring[:, b % RING, u * HALF:(u + 1) * HALF], ACT.Copy).then_inc(w2_rounded, 1)

                def y_moved(e, i):
                    n = l * N_EXP + e
                    act.wait_ge(y_mm, i * 2 + (n + 1))
                    if n >= 2:
                        act.wait_ge(y_out[e % 2], i * 16 + 16 * (n // 2))
                    A(ybuf[e % 2][:, 0:HALF], ps[:, 2, :], ACT.Copy).then_inc(y_act, 1)

                def turn(e, i, more=True):
                    w2_rounds(e - 1, i)
                    silu(e, i)
                    y_moved(e - 1, i)
                    if more:
                        xT_moved(e + 1, i)
                    aT_moved(e, i)

                xT_moved(0, 0)
                silu(0, 0)
                xT_moved(1, 0)
                aT_moved(0, 0)
                turn(1, 0)
                turn(2, 0)
                with act.Fori(0, (N_EXP - 4) // 2) as i:
                    turn(3, i)
                    turn(4, i)
                turn(N_EXP - 1, 0, more=False)
                w2_rounds(N_EXP - 1, 0)
                y_moved(N_EXP - 1, 0)

            def ov_tile(l):
                def tile(t, _):
                    act.wait_ge(ov_pe[l], 4 * t + 1)
                    A(xgT[0], ps[:, 4:6, :].rearrange("p b (k c) -> p (b k) c", k=4), ACT.Copy).then_inc(ov_act[l], 1)
                    act.wait_ge(ov_pe[l], 4 * t + 2)
                    A(s1, ps[:, 0, :], ACT.Silu).then_inc(ov_act[l], 1)
                    act.wait_ge(ov_pe[l], 4 * t + 3)
                    A(ov_actT, ps[:, 6, :].rearrange("p (k c) -> p k c", k=KF), ACT.Copy).then_inc(ov_act[l], 1)
                    act.wait_ge(ov_pe[l], 4 * t + 4)
                    A(ybuf[0].rearrange("p (b c) -> p b c", b=2), ps[:, 2:4, :], ACT.Copy).then_inc(ov_act[l], 1)
                return tile

            def combine(l, tiles):
                for t in tiles:
                    act.wait_ge(yg_in[t], 32 * (l + 1))
                    A(yg[t][:, 0, :], yg[t][:, 0, :], ACT.Copy, scale=rw[:, t, 0:1]).then_inc(comb_mul, 1)

            act.dma_start(lg[:, 3, :], g["ret_decay"].rearrange("l s h -> (l s h)").partition_broadcast(P)).then_inc(in_decay, 16)
            act.dma_start(C[:], g["consts"]).then_inc(in_tables, 16)
            for t in range(NT):
                src = g["x"][0, t * P:(t + 1) * P] if t < LT else g["ctx"][0, (t - LT) * P:(t - LT + 1) * P]
                act.dma_start(X[:, t, :], src).then_inc(in_x, 16)
            act.wait_ge(in_c, 32)
            A(c_col[:].rearrange("p k s -> p s k"), c_raw[:], ACT.Silu).then_inc(silu_c, 1)
            act.wait_ge(decay_u, 1)
            A(lgt[:, 0, :], lgt[:, 0, :], ACT.Exp, scale=-1.0).then_inc(decay_u, 1)
            act.wait_ge(in_x, 16 * NT)
            act.wait_ge(eps_set, 1)
            for l in range(DEPTH):
                nq = q_tiles(l)
                if l:
                    combine(0, (0, 1))
                norm_stat(l, "norm1", 0)
                norm_stat(l, "norm1", 1)
                cols_moved(l, 0)
                if l:
                    combine(0, (2,))
                norm_stat(l, "norm1", 2)
                cols_moved(l, 1)
                act.wait_ge(w_used, win_block(l, 0))
                win_rounds(l, 0, range(WIN_UNITS))
                if l:
                    combine(0, (3,))
                norm_stat(l, "norm1", 3)
                win_rounds(l, 0, range(WIN_UNITS, KD))
                cols_moved(l, 2)
                cols_moved(l, 3)
                if l == 0:
                    act.wait_ge(mod_out_first, 32)
                    act.wait_ge(rpb_out, 16)
                win_rounds(l, 1)
                win_rounds(l, 2)
                std_after = next(i for i, (n, _) in enumerate(PROJ[l]) if n == 2)
                for i, (n, t) in enumerate(PROJ[l]):
                    job = PROJ_BEFORE[l] + i
                    if 1 <= n < N_WIN - 1 and PROJ[l][i - 1][0] != n:
                        win_rounds(l, n + 2)
                    if i == std_after:
                        act.wait_ge(qk_ss, NT * (l + 1))
                        A(hr[:, :, 0:8], hss[:, :, 0:8], ACT.Sqrt, bias=eps[:], scale=1.0 / HD).then_inc(qk_std, 1)
                    if job % 2 == 0:
                        act.wait_ge(proj_mm, job + 1)
                        for lo, hi in needed(l, t, n):
                            last = A(z[:, t, n * HALF + lo:n * HALF + hi], ps[:, proj_bank(n, t), lo:hi], ACT.Copy)
                        last.then_inc(proj_act, 1)

                def pairs_moved(group):
                    for i, (_, is_q) in enumerate(PAIRS[group]):
                        job = l * N_PAIRS + PAIR_FIRST[group] + i
                        if job % 2 == 0:
                            cols = P * (nq if is_q else NT)
                            act.wait_ge(pair_mm, job + 1)
                            A(T[:, PAIR_SLOT[group] + i, 0:cols], ps[:, 2 + job % 4, 0:cols], ACT.Copy,
                              scale=HD ** -0.5 if group == "N" and is_q else 1.0).then_inc(pair_act, 1)

                pairs_moved("A")
                pairs_moved("N")
                attention(l)
                pairs_moved("R")
                retention(l)
                merged = sum(q_tiles(m) for m in range(l))
                act.wait_ge(ro_ev, (l + 1) * N_RH)
                act.wait_ge(o_ev, UNITS_BEFORE[l] + len(UNITS[l]))

                def merge_squares(t):
                    sq = T[:, 2 * t:2 * t + 2, :].rearrange("p a b -> p (a b)")
                    for c0, d0, w in MERGED:
                        last = A(sq[:, d0:d0 + w], z[:, t, c0:c0 + w], ACT.Square)
                    last.then_inc(mg_sq, 1)

                merge_squares(0)
                for t in range(nq):
                    if t + 1 < nq:
                        merge_squares(t + 1)
                    act.wait_ge(mg_ss, merged + t + 1)
                    A(hr[:, t, :], hss[:, t, :], ACT.Sqrt, bias=eps[:], scale=1.0 / HD).then_inc(mg_std, 1)
                for t in range(nq):
                    rows_moved(ROWS_BEFORE[l, "merge"] + t, t)
                norm_stat(l, "norm2", 0)
                norm_stat(l, "norm2", 1)
                norm(l, "norm2", nq)
                act.wait_ge(rt_max, l + 1)
                A(rtmp[:, 0:nq * N_EXP], rtmp[:, 0:nq * N_EXP], ACT.Exp).then_inc(rt_exp, 1)
                moe(l)
                overflow(act, l, ov_tile(l), lambda: act.wait_ge(y_out[1], 16 * (l + 1) * N_EXP // 2))
            for t in range(LT):
                combine(1, (t,))
            for t in range(LT):
                act.wait_ge(moe_x, q_tiles(0) + t + 1)
                square_sqrt(X[:, t, :], rowbuf[:, t, :], NORMS_BEFORE["final"] + t)

        @block.vector
        def _(dve):
            V = nc.vector
            step = [0]

            def link(ins):
                step[0] += 1
                ins.then_inc(dve_step, 1)
                dve.wait_ge(dve_step, step[0])

            def tt(o, a, b, op):
                return V.tensor_tensor(o, a, b, op)

            def heads(ap):
                return ap.rearrange("p (h d) -> p h d", d=HD)

            def norm_rows(k, streams):
                dve.wait_ge(in_rows, 16 * ROW_LOADS[k])
                for s in range(streams):
                    link(V.scalar_tensor_tensor(out=rows[2 * s], in0=rows[2 * s], scalar=1.0, in1=rows[4],
                                                op0=ALU.add, op1=ALU.mult))

            def norm_row(l, what, t):
                n, k, s = ROWS_BEFORE[l, what] + t, NORMS_BEFORE[l, what] + t, t // LT
                dve.wait_ge(row_std, k + 1)
                link(V.reciprocal(rstd[:, k:k + 1], rstd[:, k:k + 1]))
                link(V.scalar_tensor_tensor(out=rowbuf[:, n % 2, :], in0=X[:, t, :], scalar=rstd[:, k:k + 1],
                                            in1=rows[2 * s], op0=ALU.mult, op1=ALU.mult))
                tt(rowbuf[:, n % 2, :], rowbuf[:, n % 2, :], rows[2 * s + 1], ALU.add).then_inc(row_ready, 1)

            def norm_cols(l):
                dve.wait_ge(in_cols, 16 * 5 * (l + 1))
                V.scalar_tensor_tensor(out=cols[:, 0, :], in0=cols[:, 0, :], scalar=1.0, in1=cols[:, 4, :],
                                       op0=ALU.add, op1=ALU.mult)
                V.scalar_tensor_tensor(out=cols[:, 2, :], in0=cols[:, 2, :], scalar=1.0, in1=cols[:, 4, :],
                                       op0=ALU.add, op1=ALU.mult).then_inc(cols_ready, 1)
                dve.wait_ge(cols_ready, l + 1)

            def scaled_row(l, t):
                n, k = ROWS_BEFORE[l, "norm1"] + t, NORMS_BEFORE[l, "norm1"] + t
                dve.wait_ge(row_std, k + 1)
                link(V.reciprocal(rstd[:, k:k + 1], rstd[:, k:k + 1]))
                V.tensor_scalar(rowbuf[:, n % 2, :], X[:, t, :], rstd[:, k:k + 1], None, ALU.mult).then_inc(row_ready, 1)

            def cols_moved(l, t):
                n, s = ROWS_BEFORE[l, "norm1"] + t, 2 * (t // LT)
                dve.wait_ge(rowT_mm, 2 * n + 2)
                row = rowbuf[:, n % 2, :].rearrange("p (k c) -> p k c", k=KD)
                for k in range(4):
                    last = V.tensor_scalar(row[:, 4 + k, :], ps[:, 3 + 2 * (n % 2), k * P:(k + 1) * P],
                                           cols[:, s, 4 + k:5 + k], cols[:, s + 1, 4 + k:5 + k], ALU.mult, ALU.add)
                last.then_inc(rowT_dve, 1)
                dve.wait_ge(h_round, NT * l + t + 1)
                tt(h_lo[:, :, t * P:(t + 1) * P], row, h_hi[:, :, t * P:(t + 1) * P].bitcast(F32),
                   ALU.subtract).then_inc(h_split, 1)

            def win_rests(l, i, chunks=range(KD)):
                n = PASSES[i][0]
                b, c = win_block(l, n), win_cols(n)
                for k in chunks:
                    u = (len(PASSES) * l + i) * KD + k
                    dve.wait_ge(win_rounded, u + 1)
                    tt(win_lo[:, u % WIN_UNITS, 0:c], ring[:, b % RING, k * c:(k + 1) * c],
                       win_hi[:, u % WIN_UNITS, 0:c].bitcast(F32), ALU.subtract).then_inc(win_split, 1)

            def rows_moved(n, t):
                dve.wait_ge(rowT_mm, 2 * n + 2)
                V.tensor_copy(T[:, 4:8, t * P:(t + 1) * P],
                              ps[:, 3 + 2 * (n % 2), :].rearrange("p (k c) -> p k c", k=4)).then_inc(rowT_dve, 1)

            def ada_moved(jobs, bank0=0):
                for job in jobs:
                    if job < N_FIRST:
                        dve.wait_ge(in_brow_first, 16)
                    else:
                        dve.wait_ge(in_brow[job % 2], 16 * row_uses(job))
                    dve.wait_ge(w_used, ADA_BLOCK[job] + 1)
                    tt(modrow(job), ps[0:2, bank0 + job % 2, :], modrow(job), ALU.add).then_inc(ada_ev, 1)

            def qk_squares(l, t):
                h0 = 0 if t < q_tiles(l) else 6
                sq = R2[:, 0, HD * h0:HALF]
                link(tt(sq, z[:, t, HD * h0:HALF], z[:, t, HD * h0:HALF], ALU.mult))
                V.tensor_reduce(hss[:, t, h0:8], heads(sq), X_AXIS, ALU.add).then_inc(qk_ss, 1)
                dve.wait_ge(qk_ss, NT * l + t + 1)

            def qk_norm(l, t):
                h0 = 0 if t < q_tiles(l) else 6
                v, normed = z[:, t, HD * h0:HALF], R2[:, 0, HD * h0:HALF]
                link(tt(heads(normed), heads(v), hr[:, t, h0:8].unsqueeze(2).to_broadcast([P, 8 - h0, HD]), ALU.mult))
                if h0 == 0:
                    link(tt(z[:, t, 0:A_K].rearrange("p (i g d) -> p g i d", g=2, d=HD),
                            R2[:, 0, 0:A_K].rearrange("p (g i d) -> p g i d", g=2, d=HD),
                            qk_gain[:, l, 0, :].unsqueeze(1).unsqueeze(1).to_broadcast([P, 2, 3, HD]), ALU.mult))
                ins = tt(heads(z[:, t, A_K:A_V]), heads(R2[:, 0, A_K:A_V]),
                         qk_gain[:, l, 1, :].unsqueeze(1).to_broadcast([P, 2, HD]), ALU.mult)
                if t < LT:
                    link(ins)
                    cos, sin = const("cos")[:, HD * t:HD * (t + 1)], const("sin")[:, HD * t:HD * (t + 1)]
                    by_cos, by_sin = R2[:, 0, 0:HALF], R2[:, 0, HALF:]
                    link(tt(heads(by_cos), heads(v), cos.unsqueeze(1).to_broadcast([P, 8, HD]), ALU.mult))
                    zv, sv = (x.rearrange("p (h f j i) -> p h f j i", h=8, f=2, j=2) for x in (v, by_sin))
                    sn = sin.rearrange("p (f j i) -> p f j i", f=2, j=2)
                    for j in range(2):
                        link(tt(sv[:, :, :, j, :], zv[:, :, :, 1 - j, :],
                                sn[:, :, j, :].unsqueeze(1).to_broadcast([P, 8, 2, 16]), ALU.mult))
                    ins = tt(v, by_cos, by_sin, ALU.add)
                ins.then_inc(qk_ready, 1)
                dve.wait_ge(qk_ready, NT * l + t + 1)

            def projection(l):
                if l == 0:
                    dve.wait_ge(mod_out_first, 32)
                    dve.wait_ge(rpb_out, 16)
                win_rests(l, 1)
                win_rests(l, 2)
                first = {n: next(i for i, (m, _) in enumerate(PROJ[l]) if m == n) for n in range(N_WIN)}
                for i, (n, t) in enumerate(PROJ[l]):
                    job = PROJ_BEFORE[l] + i
                    if 1 <= n < N_WIN - 1 and i == first[n]:
                        win_rests(l, n + 2)
                    if i == first[2]:
                        dve.wait_ge(proj_act, (PROJ_BEFORE[l] + first[1] + 1) // 2)
                        for tile in range(NT):
                            qk_squares(l, tile)
                    if i == first[3]:
                        dve.wait_ge(qk_std, l + 1)
                        link(V.reciprocal(hr[:, :, 0:8], hr[:, :, 0:8]))
                        for tile in range(LT):
                            qk_norm(l, tile)
                    if i == first[4]:
                        for tile in range(LT, NT):
                            qk_norm(l, tile)
                    if job % 2 == 1:
                        dve.wait_ge(proj_mm, job + 1)
                        for lo, hi in needed(l, t, n):
                            last = V.tensor_copy(z[:, t, n * HALF + lo:n * HALF + hi], ps[:, proj_bank(n, t), lo:hi])
                        last.then_inc(proj_dve, 1)

            def bias(l):
                dve.wait_ge(in_bias, 16 * 16 * (l + 1))
                v = R3[:].rearrange("p a b -> p (a b)").rearrange("p (n k) -> p n k", k=GRID_W)
                tt(v, v, const("mask").unsqueeze(1).to_broadcast([P, 32, GRID_W]), ALU.add).then_inc(bias_ready, 1)

            def pairs_moved(l, group):
                for i, (_, is_q) in enumerate(PAIRS[group]):
                    job = l * N_PAIRS + PAIR_FIRST[group] + i
                    if job % 2 == 1:
                        cols = P * (q_tiles(l) if is_q else NT)
                        dve.wait_ge(pair_mm, job + 1)
                        o, src = T[:, PAIR_SLOT[group] + i, 0:cols], ps[:, 2 + job % 4, 0:cols]
                        if group == "N" and is_q:
                            V.tensor_scalar(o, src, HD ** -0.5, None, ALU.mult).then_inc(pair_dve, 1)
                        else:
                            V.tensor_copy(o, src).then_inc(pair_dve, 1)

            def attention(l):
                us, before = UNITS[l], UNITS_BEFORE[l]

                def maximum(i):
                    n, cols = before + i, P * len(us[i]["keys"])
                    dve.wait_ge(score_mm, n + 1)
                    V.tensor_reduce(soft[:, 0, n % 4:n % 4 + 1], ps[:, SCORE_BANK[n % 3], 0:cols], X_AXIS, ALU.max,
                                    negate=True).then_inc(max_ready, 1)

                def output(i):
                    u, n = us[i], before + i
                    dve.wait_ge(o_mm, n + 1)
                    link(V.reciprocal(soft[:, 2, n % 4:n % 4 + 1], soft[:, 1, n % 4:n % 4 + 1]))
                    V.tensor_scalar(z[:, u["t"], u["o"]:u["o"] + HD], ps[:, 4 + n % 2, 0:HD],
                                    soft[:, 2, n % 4:n % 4 + 1], None, ALU.mult).then_inc(o_ev, 1)

                maximum(0)
                maximum(1)
                for i in range(len(us) + 1):
                    if i == 6 * q_tiles(l) - 4:
                        bias(l)
                    if i + 2 < len(us):
                        maximum(i + 2)
                    if i >= 1:
                        output(i - 1)

            def retention(l):
                jobs, nj = ret_jobs(l), len(ret_jobs(l))

                def tables(r):
                    head = l * N_RH + r
                    near, far = near_tab[r % 2], far_tab[r % 2]
                    dve.wait_ge(decay_exp, 4 * (head + 1))
                    link(tt(near, near, T[:, 6, 0:LAGS], ALU.mult))
                    link(tt(far, far, T[:, 7, 0:LAGS], ALU.add))
                    tt(near[:, P:2 * P], near[:, P:2 * P], ident, ALU.add).then_inc(w_ready, 1)
                    dve.wait_ge(w_ready, head + 1)

                def windows(r, table):
                    v = (near_tab if table == "near" else far_tab)[r % 2][:, 0:256]
                    return bass.AP(v.tensor, v.offset, [v.ap[0], [P, 2], [1, 256]])

                def weighted(r):
                    for j, (_, _, table) in enumerate(jobs):
                        job = RJ_BEFORE[l] + r * nj + j
                        dve.wait_ge(rscore_mm, job + 1)
                        before = r * nj + j - 4
                        if before >= 0:
                            dve.wait_ge(ro_mm, l * N_RH + before // nj + 1)
                        o = R2[:, (job % 4) // 2, (job % 2) * HALF:(job % 2 + 1) * HALF]
                        V.scalar_tensor_tensor(out=o.rearrange("p (k c) -> p k c", k=2),
                                               in0=ps[:, RET_BANK[j], :].rearrange("p (k c) -> p k c", k=2),
                                               scalar=HD ** -0.5, in1=windows(r, table), op0=ALU.mult, op1=ALU.mult).then_inc(rscore_w, 1)
                    dve.wait_ge(rscore_w, RJ_BEFORE[l] + (r + 1) * nj)

                tables(0)
                for r in range(N_RH):
                    weighted(r)
                    if r + 1 < N_RH:
                        tables(r + 1)
                    if l == 0:
                        ada_moved([ADA_RET[r]], 2)

            def merge_sums(l, t):
                n = sum(q_tiles(m) for m in range(l)) + t
                dve.wait_ge(mg_sq, n + 1)
                sq = T[:, 2 * t:2 * t + 2, :].rearrange("p a b -> p (a b)")
                V.tensor_reduce(hss[:, t, :], heads(sq), X_AXIS, ALU.add).then_inc(mg_ss, 1)

            def merge_row(l, t):
                n = ROWS_BEFORE[l, "merge"] + t
                row = rowbuf[:, n % 2, :]
                dve.wait_ge(rowT_mm, 2 * (n - 1))
                dve.wait_ge(mg_std, sum(q_tiles(m) for m in range(l)) + t + 1)
                link(V.reciprocal(hr[:, t, :], hr[:, t, :]))
                for c0, d0, w in MERGED:
                    link(tt(heads(row[:, d0:d0 + w]), heads(z[:, t, c0:c0 + w]),
                            hr[:, t, d0 // HD:(d0 + w) // HD].unsqueeze(2).to_broadcast([P, w // HD, HD]), ALU.mult))
                link(tt(row, row, R3[:, 0, :], ALU.mult))
                tt(row[:, 640:], row[:, 640:], z[:, t, R_G:], ALU.mult).then_inc(row_ready, 1)

            def x_update(l, t):
                for half in range(2):
                    job = 2 * (NT * l + t) + half
                    tmp, cols = R3[:, 1, half * HALF:(half + 1) * HALF], slice(half * HALF, (half + 1) * HALF)
                    dve.wait_ge(wout_mm, job + 1)
                    link(tt(tmp, ps[:, 6 + half, :], R1[:, t // LT, cols], ALU.mult))
                    tt(X[:, t, cols], X[:, t, cols], tmp, ALU.add).then_inc(x_upd, 1)
                dve.wait_ge(x_upd, 2 * (NT * l + t) + 2)

            def routing(l):
                nq = q_tiles(l)
                w = nq * N_EXP
                free = [w]

                def new(cols):
                    a = free[0]
                    free[0] += cols
                    return rtmp[:, a:a + cols]

                def by(ap, k):
                    return ap.rearrange("p (n e) -> p n e", e=k)

                def wide(ap, k):
                    return ap.unsqueeze(2).to_broadcast([P, ap.shape[1], k])

                def reduce(v, k, op):
                    o = new(v.shape[1] // k)
                    link(V.tensor_reduce(o, by(v, k), X_AXIS, op))
                    return o

                def first_of_max(v, k, order):
                    top = reduce(v, k, ALU.max)
                    at, o = new(v.shape[1]), new(v.shape[1])
                    link(tt(by(at, k), by(v, k), wide(top, k), ALU.is_equal))
                    link(tt(by(at, k), by(at, k), order.unsqueeze(1).to_broadcast([P, v.shape[1] // k, k]), ALU.mult))
                    lead = reduce(at, k, ALU.max)
                    link(tt(by(o, k), by(at, k), wide(lead, k), ALU.is_equal))
                    return o, top

                dve.wait_ge(rt_mm, l + 1)
                p = rtmp[:, 0:w]
                link(tt(by(p, N_EXP), ps[:, 6, 0:w].rearrange("p (n e) -> p n e", e=N_EXP),
                        b_rt[:].unsqueeze(1).to_broadcast([P, nq, N_EXP]), ALU.add))
                m = reduce(p, N_EXP, ALU.max)
                tt(by(p, N_EXP), by(p, N_EXP), wide(m, N_EXP), ALU.subtract).then_inc(rt_max, 1)
                dve.wait_ge(rt_exp, l + 1)
                s = reduce(p, N_EXP, ALU.add)
                link(V.reciprocal(s, s))
                link(tt(by(p, N_EXP), by(p, N_EXP), wide(s, N_EXP), ALU.mult))
                g4 = p.rearrange("p (n i) -> p n i", i=4)
                hi1, lo1, hi2, lo2 = (new(nq * 4) for _ in range(4))
                link(tt(hi1, g4[:, :, 0], g4[:, :, 1], ALU.max))
                link(tt(lo1, g4[:, :, 0], g4[:, :, 1], ALU.min))
                link(tt(hi2, g4[:, :, 2], g4[:, :, 3], ALU.max))
                link(tt(lo2, g4[:, :, 2], g4[:, :, 3], ALU.min))
                link(tt(lo1, lo1, lo2, ALU.max))
                link(tt(lo2, hi1, hi2, ALU.min))
                link(tt(hi1, hi1, hi2, ALU.max))
                link(tt(lo1, lo1, lo2, ALU.max))
                link(tt(hi1, hi1, lo1, ALU.add))
                chosen, _ = first_of_max(hi1, 4, const("down")[:, 0:4])
                cand = new(w)
                link(tt(by(cand, 4), g4, wide(chosen, 4), ALU.mult))
                oh1, m1 = first_of_max(cand, N_EXP, const("down"))
                link(V.scalar_tensor_tensor(out=cand, in0=oh1, scalar=-2.0, in1=cand, op0=ALU.mult, op1=ALU.add))
                oh2, m2 = first_of_max(cand, N_EXP, const("down"))
                link(tt(rtmp[:, 0:w], oh1, oh2, ALU.add))
                s2 = new(nq)
                link(tt(s2, m1, m2, ALU.add))
                link(V.reciprocal(s2, s2))
                link(tt(rw[:, 0:nq, 0], m1, s2, ALU.mult))
                tt(rw[:, 0:nq, 1], m2, s2, ALU.mult).then_inc(rt_sel, 1)
                return oh1, oh2, new, by, reduce

            def slot_numbers(l, oh1, oh2, new, by, reduce):
                nq = q_tiles(l)
                w = nq * N_EXP
                dve.wait_ge(rank_mm, l + 1)
                rank, q, t1, ge1 = (new(w + N_EXP) for _ in range(4))
                link(V.tensor_copy(rank, ps[:, 7, 0:w + N_EXP]))
                link(V.tensor_scalar(rank[:, w:], rank[:, w:], -1.0, None, ALU.add))
                link(V.tensor_scalar(ge1, rank, 128.0, None, ALU.is_ge))
                link(V.tensor_scalar(q, rank, 256.0, None, ALU.is_ge))
                link(V.tensor_scalar(t1, rank, 384.0, None, ALU.is_ge))
                link(tt(q, q, t1, ALU.add))
                link(tt(q, q, ge1, ALU.add))
                a, b = new(N_EXP), new(N_EXP)
                link(V.tensor_copy(a, q[:, w:]))
                for s in (1, 2, 4, 8):
                    link(V.tensor_copy(b[:, 0:s], a[:, 0:s]))
                    link(tt(b[:, s:], a[:, s:], a[:, 0:N_EXP - s], ALU.add))
                    a, b = b, a
                base = new(N_EXP)
                link(tt(base, a, q[:, w:], ALU.subtract))
                link(V.scalar_tensor_tensor(out=base, in0=base, scalar=15.0, in1=const("up"), op0=ALU.add, op1=ALU.subtract))
                addr = rank[:, 0:w]
                link(V.tensor_scalar(addr, addr, float(SLOT_T[l]), None, ALU.mult))
                link(V.scalar_tensor_tensor(out=addr, in0=q[:, 0:w], scalar=1.0 - SLOT_T[l] * P, in1=addr,
                                            op0=ALU.mult, op1=ALU.add))
                every = [P, nq, N_EXP]
                link(tt(by(ge1[:, 0:w], N_EXP), by(ge1[:, 0:w], N_EXP), base.unsqueeze(1).to_broadcast(every), ALU.mult))
                link(tt(addr, addr, ge1[:, 0:w], ALU.add))
                link(tt(by(addr, N_EXP), by(addr, N_EXP), const("up").unsqueeze(1).to_broadcast(every), ALU.add))
                for k, oh in enumerate((oh1, oh2)):
                    link(tt(oh, oh, addr, ALU.mult))
                    s = reduce(oh, N_EXP, ALU.add)
                    link(V.tensor_copy(slots[:, 0:nq, k], s))
                n_ov, over = OV_MAX[0], new(OV_MAX[0] * N_EXP)
                v = over[0:1, :].rearrange("p (t e) -> p t e", e=N_EXP)
                link(tt(v, a[0:1, :].unsqueeze(1).to_broadcast([1, n_ov, N_EXP]),
                        const("up")[0:1, 0:n_ov].unsqueeze(2).to_broadcast([1, n_ov, N_EXP]), ALU.is_le))
                e = new(TOP)
                link(V.tensor_reduce(e[0:1, 1:TOP], v, X_AXIS, ALU.add))
                link(V.tensor_scalar(e[0:1, 1:TOP], e[0:1, 1:TOP], float(N_EXP - 1), None, ALU.min))
                link(V.tensor_copy(e[0:1, 0:1], a[0:1, N_EXP - 1:N_EXP]))
                V.tensor_copy(ovinfo[:], e[0:1, :]).then_inc(slots_ready, 1)

            def moe(l):
                def xT_moved(e, i):
                    n = l * N_EXP + e
                    dve.wait_ge(xT_mm, i * 4 + (2 * n + 2))
                    V.tensor_copy(xgT[e % 2][:, 4:8, :],
                                  ps[:, 5, :].rearrange("p (k c) -> p k c", k=4)).then_inc(xT_dve, 1)

                def gated(e, i):
                    n = l * N_EXP + e
                    dve.wait_ge(w_used, i * RING + (moe_block(l, e, 1) + 1))
                    dve.wait_ge(silu_h, i * 2 + (n + 1))
                    if n:
                        dve.wait_ge(aT_mm, i * 2 + n)
                    tt(act_sb, s1, ps[:, 1, :], ALU.mult).then_inc(act_ready, 1)

                def y_moved(e, i):
                    n = l * N_EXP + e
                    dve.wait_ge(w_used, i * RING + (moe_block(l, e, 2) + 1))
                    if n >= 2:
                        dve.wait_ge(y_out[e % 2], i * 16 + 16 * (n // 2))
                    V.tensor_copy(ybuf[e % 2][:, HALF:], ps[:, 3, :]).then_inc(y_dve, 1)

                def w2_rests(e, i):
                    n, b = l * N_EXP + e, moe_block(l, e, 2)
                    for u in range(2 * KF):
                        at = slice(u % 2 * HALF, (u % 2 + 1) * HALF)
                        dve.wait_ge(w2_rounded, i * 4 * KF + (2 * KF * n + u + 1))
                        tt(w2_lo[:, u % 4 // 2, at], ring[:, b % RING, u * HALF:(u + 1) * HALF],
                           w2_hi[:, u % 4 // 2, at].bitcast(F32), ALU.subtract).then_inc(w2_split, 1)

                def actT_rest(e, i):
                    n = l * N_EXP + e
                    dve.wait_ge(aT_hi, i * 2 + (n + 1))
                    tt(actT_lo[:, e % 2, :, :].rearrange("p k c -> p (k c)"), ps[:, 6, :],
                       actT_hi[:, e % 2, :, :].rearrange("p k c -> p (k c)").bitcast(F32), ALU.subtract).then_inc(aT_ev, 1)

                def turn(e, i, more=True):
                    w2_rests(e - 1, i)
                    y_moved(e - 1, i)
                    gated(e, i)
                    if more:
                        xT_moved(e + 1, i)
                    actT_rest(e, i)

                xT_moved(0, 0)
                gated(0, 0)
                xT_moved(1, 0)
                actT_rest(0, 0)
                turn(1, 0)
                turn(2, 0)
                with dve.Fori(0, (N_EXP - 4) // 2) as i:
                    turn(3, i)
                    turn(4, i)
                turn(N_EXP - 1, 0, more=False)
                w2_rests(N_EXP - 1, 0)
                y_moved(N_EXP - 1, 0)

            def ov_tile(l):
                def tile(t, _):
                    dve.wait_ge(ov_act[l], 4 * t + 2)
                    tt(act_sb, s1, ps[:, 1, :], ALU.mult).then_inc(ov_dve[l], 1)
                return tile

            def combine(l, tiles):
                done = sum(q_tiles(m) for m in range(l))
                dve.wait_ge(in_gate, 32 * (2 * l + 2))
                for t in tiles:
                    dve.wait_ge(comb_mul, done + t + 1)
                    y0, y1 = yg[t][:, 0, :], yg[t][:, 1, :]
                    link(V.scalar_tensor_tensor(out=y0, in0=y1, scalar=rw[:, t, 1:2], in1=y0, op0=ALU.mult, op1=ALU.add))
                    link(tt(y0, y0, moe_gate[t // LT], ALU.mult))
                    tt(X[:, t, :], X[:, t, :], y0, ALU.add).then_inc(moe_x, 1)

            V.memset(rpb_pad, 0.0).then_inc(pad_zero, 1)
            V.memset(hss[:], 1.0).then_inc(pad_zero, 1)
            V.memset(eps[:], EPS).then_inc(eps_set, 1)
            nl = 2 * DEPTH * N_RH
            dve.wait_ge(in_decay, 16)
            x, t0, t1, acc = lg[:, 3, :], lgt[:, 0, :], lgt[:, 1, :], lg[:, 0, :]
            link(V.tensor_scalar(t0, x, -1.0, None, ALU.mult))
            tt(t0, t0, x, ALU.max).then_inc(decay_u, 1)
            dve.wait_ge(decay_u, 2)
            link(V.tensor_scalar(t1, t0, 2.0, None, ALU.add))
            link(V.reciprocal(t1, t1))
            link(tt(t0, t0, t1, ALU.mult))
            link(tt(t1, t0, t0, ALU.mult))
            link(V.memset(acc, 0.0))
            for n in range(17, 1, -2):
                link(V.scalar_tensor_tensor(out=acc, in0=acc, scalar=1.0 / n, in1=t1, op0=ALU.add, op1=ALU.mult))
            link(V.scalar_tensor_tensor(out=acc, in0=acc, scalar=1.0, in1=t0, op0=ALU.add, op1=ALU.mult))
            link(V.tensor_scalar(x, x, 0.0, None, ALU.min))
            link(V.scalar_tensor_tensor(out=acc, in0=acc, scalar=-2.0, in1=x, op0=ALU.mult, op1=ALU.add))
            link(V.tensor_scalar(lg[:, 1, :], acc, -1.0, None, ALU.mult))
            link(V.tensor_scalar(lg[:, 2, :], acc, 256.0, None, ALU.mult))
            ada_moved(ADA_START)
            for l in range(DEPTH):
                nq = q_tiles(l)
                n = ROWS_BEFORE[l, "norm1"]
                if l == 0:
                    ada_moved(ADA_NORM)
                    scaled_row(l, 0)
                    scaled_row(l, 1)
                    norm_cols(0)
                    dve.wait_ge(in_tables, 16)
                    dve.wait_ge(in_const, 16 * N_CONST_LOADS)
                    link(V.tensor_scalar(qk_gain[:, :, 0, :], qk_gain[:, :, 0, :], HD ** -0.5, None, ALU.mult))
                else:
                    combine(0, (0,))
                    ada_moved(ADA_COMBINE)
                    dve.wait_ge(mod_out[ADA_COMBINE[-1] % 2], 16 * row_uses(ADA_COMBINE[-1]))
                    norm_cols(1)
                    combine(0, (1,))
                    scaled_row(l, 0)
                    scaled_row(l, 1)
                for t in range(NT):
                    cols_moved(l, t)
                    if t == 1:
                        win_rests(l, 0, range(WIN_UNITS))
                    if t + 2 < NT:
                        if l:
                            combine(0, (t + 2,))
                        scaled_row(l, t + 2)
                    if t == 1:
                        win_rests(l, 0, range(WIN_UNITS, KD))
                projection(l)
                dve.wait_ge(proj_mm, PROJ_BEFORE[l] + len(PROJ[l]))
                V.tensor_scalar(behind, const("lag"), 0.0, None, ALU.min).then_inc(behind_ready, 1)
                pairs_moved(l, "A")
                pairs_moved(l, "N")
                attention(l)
                pairs_moved(l, "R")
                retention(l)
                dve.wait_ge(ro_ev, (l + 1) * N_RH)
                dve.wait_ge(o_ev, UNITS_BEFORE[l] + len(UNITS[l]))
                n = ROWS_BEFORE[l, "merge"]
                n2 = ROWS_BEFORE[l, "norm2"]
                merge_sums(l, 0)
                dve.wait_ge(silu_g, l + 1)
                dve.wait_ge(in_mix, 16 * (l + 1))
                merge_row(l, 0)
                for t in range(1, nq):
                    merge_sums(l, t)
                merge_row(l, 1)
                ada_moved(ADA_MERGE[l])
                rows_moved(n, 0)
                rows_moved(n + 1, 1)
                for t in range(2, nq):
                    merge_row(l, t)
                dve.wait_ge(in_gate, 32 * (2 * l + 1))
                for job in ADA_MERGE[l]:
                    dve.wait_ge(mod_out[job % 2], 16 * row_uses(job))
                x_update(l, 0)
                if nq > 2:
                    rows_moved(n + 2, 2)
                    x_update(l, 1)
                    rows_moved(n + 3, 3)
                norm_rows(l, nq // LT)
                norm_row(l, "norm2", 0)
                x_update(l, nq - 2 if nq > 2 else 1)
                norm_row(l, "norm2", 1)
                if nq > 2:
                    x_update(l, 3)
                for t in range(nq):
                    rows_moved(n2 + t, t)
                    if t + 2 < nq:
                        norm_row(l, "norm2", t + 2)
                parts = routing(l)
                ada_moved(ADA_ROUTE[l])
                slot_numbers(l, *parts)
                ada_moved(ADA_SLOTS[l])
                moe(l)
                overflow(dve, l, ov_tile(l), lambda: dve.nop())
            combine(1, range(LT))
            dve.wait_ge(fin_in, 16)
            for t in range(LT):
                k = NORMS_BEFORE["final"] + t
                dve.wait_ge(row_std, k + 1)
                link(V.reciprocal(rstd[:, k:k + 1], rstd[:, k:k + 1]))
                V.scalar_tensor_tensor(out=rowbuf[:, t, :], in0=X[:, t, :], scalar=rstd[:, k:k + 1], in1=R3[:, 0, :],
                                       op0=ALU.mult, op1=ALU.mult).then_inc(fin_ready, 1)

        @block.gpsimd
        def _(pool):
            dma = pool.dma_start

            def bcast(ap, n=P):
                return ap.partition_broadcast(n)

            def brow(job):
                src = g["b_ada"][job // N_ADA, (job % N_ADA) * HALF:(job % N_ADA + 1) * HALF]
                dma(modrow(job), bcast(src, 2)).then_inc(in_brow[job % 2], 16)

            def modulation_out(jobs):
                for job in jobs:
                    pool.wait_ge(ada_ev, job + 1)
                    l, n = job // N_ADA, job % N_ADA
                    dma(mod_d[l, :, n * HALF:(n + 1) * HALF], modrow(job)).then_inc(mod_out[job % 2], 16)
                    pool.wait_ge(mod_out[job % 2], 16 * row_uses(job))
                    if any(first <= job and job + 2 < end for first, end in ADA_RUNS):
                        brow(job + 2)

            def norm_cols(l):
                def column(v):
                    return v.rearrange("(p k) -> p k", k=KD)

                for s in range(2):
                    dma(cols[:, 2 * s, :], column(mod_d[l, s, D:2 * D])).then_inc(in_cols, 16)
                    dma(cols[:, 2 * s + 1, :], column(mod_d[l, s, 0:D])).then_inc(in_cols, 16)
                dma(cols[:, 4, :], column(g["norm1_g"][l])).then_inc(in_cols, 16)

            def norm_rows(l, streams):
                for s in range(streams):
                    dma(rows[2 * s], bcast(mod_d[l, s, 4 * D:5 * D])).then_inc(in_rows, 16)
                    dma(rows[2 * s + 1], bcast(mod_d[l, s, 3 * D:4 * D])).then_inc(in_rows, 16)
                dma(rows[4], bcast(g["norm2_g"][l])).then_inc(in_rows, 16)

            def gates(l, k):
                for s in range(2):
                    dma(moe_gate[s] if k else R1[:, s, :], bcast(mod_d[l, s, (3 * k + 2) * D:(3 * k + 3) * D])).then_inc(in_gate, 16)

            def bias(l):
                v = R3[:].rearrange("p a b -> p (a b)").rearrange("p (h t k c) -> p h t k c", h=4, t=2, c=GRID_W)
                for t in range(2):
                    for r in range(2):
                        for h in range(4):
                            row = (l * 4 + h) * 15 + 7 - (2 * t + r)
                            dma(v[r * GRID_W:(r + 1) * GRID_W, h, t],
                                near_d[row:row + 4].rearrange("k q c -> q k c")).then_inc(in_bias, 16)

            dma(Z[0:2, 0:N_FIRST * HALF], bcast(g["b_ada"][0, 0:N_FIRST * HALF], 2)).then_inc(in_brow_first, 16)
            dma(ids[:], g["ids"]).then_inc(in_const, 16)
            dma(w_rt[:], g["w_router"].rearrange("(p k) e -> p k e", k=KD)).then_inc(in_const, 16)
            dma(b_rt[:], bcast(g["b_router"])).then_inc(in_const, 16)
            for l in range(DEPTH):
                dma(qk_gain[:, l, 0, :], bcast(g["q_norm_g"][l])).then_inc(in_const, 16)
                dma(qk_gain[:, l, 1, :], bcast(g["k_norm_g"][l])).then_inc(in_const, 16)
            pool.wait_ge(pad_zero, 1)
            dma(rpb_pad[:, 48:79], g["na_rpb"].rearrange("l h r c -> (l h r) c")).then_inc(in_rpb, 16)
            pool.wait_ge(in_rpb, 16)
            dma(rpb_d, rpb_pad).then_inc(rpb_out, 16)
            for jobs in (ADA_START, ADA_NORM):
                a, b = jobs[0] * HALF, (jobs[-1] + 1) * HALF
                pool.wait_ge(ada_ev, jobs[-1] + 1)
                dma(mod_d[0, :, a:b], Z[0:2, a:b]).then_inc(mod_out_first, 16)
                pool.wait_ge(mod_out_first, 16 if jobs == ADA_START else 32)
                if jobs == ADA_START:
                    norm_cols(0)
            pool.wait_ge(row_ready, NT)
            pool.wait_ge(in_const, 16 * N_CONST_LOADS)
            for l in range(DEPTH):
                dma(slot_d[l].rearrange("(p n) o -> p (n o)", n=SLOT_T[l]), ids[:, 0:SLOT_T[l]]).then_inc(slot_zero, 16)
            pool.wait_ge(rpb_out, 16)
            for l in range(DEPTH):
                src = bass.AP(rpb_d.tensor, l * 60 * P + 63, [[P, 60], [-1, GRID_W], [1, GRID_W]])
                dma(near_d[l * 60:(l + 1) * 60], src).then_inc(bias_spread, 16)
            for l in range(DEPTH):
                nq = q_tiles(l)
                pool.wait_ge(bias_spread, 32)
                pool.wait_ge(proj_mm, PROJ_BEFORE[l] + len(PROJ[l]))
                bias(l)
                for t in range(OV_MAX[l]):
                    dma(y_d[l].rearrange("(p n) d -> p n d", n=SLOT_T[l])[:, N_EXP + t, :], g["zeros"]).then_inc(y_zero, 16)
                pool.wait_ge(score_mm, UNITS_BEFORE[l] + len(UNITS[l]))
                for job in ADA_MERGE[1] if l else ADA_RET[0:2]:
                    brow(job)
                dma(R3[:, 0, :], bcast(g["mix_g"][l])).then_inc(in_mix, 16)
                if l == 0:
                    modulation_out(ADA_RET)
                pool.wait_ge(rscore_w, RJ_BEFORE[l] + N_RH * len(ret_jobs(l)))
                gates(l, 0)
                modulation_out(ADA_MERGE[l])
                pool.wait_ge(row_ready, ROWS_BEFORE[l, "norm2"])
                norm_rows(l, nq // LT)
                for t in range(nq):
                    n = ROWS_BEFORE[l, "norm2"] + t
                    pool.wait_ge(row_ready, n + 1)
                    dma(h2_d[l][t * P:(t + 1) * P], rowbuf[:, n % 2, :]).then_inc(h2_out[n % 2], 16)
                for job in (ADA_ROUTE[0] if l == 0 else range(22, 24)):
                    brow(job)
                pool.wait_ge(rt_mm, l + 1)
                for i in range(2):
                    pool.wait_ge(h2_out[i], h2_stored(ROWS_BEFORE[l, "norm2"] + nq, i))
                modulation_out(ADA_ROUTE[l])

                pool.wait_ge(slots_ready, l + 1)
                pool.wait_ge(slot_zero, 32)
                for t in range(nq):
                    for k in range(2):
                        pool.indirect_dma_start(slot_d[l], bass.IndirectOffsetOnAxis(ap=slots[:, t, k:k + 1], axis=0),
                                                ids[:, SLOT_T[0] + t:SLOT_T[0] + t + 1], None).then_inc(slot_out, 16)
                modulation_out(ADA_SLOTS[l][0:1])
                pool.wait_ge(slot_out, 32 * (nq + (q_tiles(0) if l else 0)))
                dma(slot_tok[:, 0:SLOT_T[l]], slot_d[l].rearrange("(p n) o -> p (n o)", n=SLOT_T[l])).then_inc(slot_in, 16)
                modulation_out(ADA_SLOTS[l][1:2])
                pool.wait_ge(slot_in, 16 * (l + 1))

                def gather(n, dst, s):
                    pool.indirect_dma_start(dst, None, h2_d[l],
                                            bass.IndirectOffsetOnAxis(ap=slot_tok[:, n:n + 1], axis=0)).then_inc(s, 16)

                y_rows = y_d[l].rearrange("(p n) d -> p n d", n=SLOT_T[l])

                def y_store(e):
                    n = l * N_EXP + e
                    pool.wait_ge(y_act, n + 1)
                    pool.wait_ge(y_dve, n + 1)
                    dma(y_rows[:, e, :], ybuf[e % 2]).then_inc(y_out[e % 2], 16)

                gather(0, xg[0], xg_in[0])
                gather(1, xg[1], xg_in[1])
                modulation_out(ADA_SLOTS[l][2:])
                if l == 0:
                    norm_cols(1)
                gates(l, 1)
                for e in range(N_EXP):
                    if e >= 2:
                        pool.wait_ge(xT_mm, 2 * (l * N_EXP + e - 1))
                        gather(e, xg[e % 2], xg_in[e % 2])
                    if e >= 3:
                        y_store(e - 3)
                for e in range(N_EXP - 3, N_EXP):
                    y_store(e)
                for i in range(2):
                    pool.wait_ge(y_out[i], 16 * (l + 1) * N_EXP // 2)

                pool.wait_ge(y_zero, 16 * sum(OV_MAX[:l + 1]))

                def ov_tile(t, _):
                    gather(N_EXP + t, xg[0], ov_xg_in[l])
                    pool.wait_ge(ov_act[l], 4 * t + 4)
                    dma(y_rows[:, N_EXP + t, :], ybuf[0]).then_inc(ov_y_out[l], 16)
                    pool.wait_ge(ov_y_out[l], 16 * (t + 1))
                    pool.nop()

                overflow(pool, l, ov_tile, lambda: pool.nop())
                for t in range(nq):
                    for k in range(2):
                        pool.indirect_dma_start(yg[t][:, k, :], None, y_d[l],
                                                bass.IndirectOffsetOnAxis(ap=slots[:, t, k:k + 1], axis=0)
                                                ).then_inc(yg_in[t], 16)
                if l == 0:
                    modulation_out(ADA_COMBINE)
                else:
                    dma(R3[:, 0, :], bcast(g["final_g"])).then_inc(fin_in, 16)
            for t in range(LT):
                pool.wait_ge(fin_ready, t + 1)
                dma(out[0, t * P:(t + 1) * P], rowbuf[:, t, :]).then_inc(res_out, 16)
            pool.wait_ge(res_out, 16 * LT)


ROW_LOADS = [5, 8]
N_CONST_LOADS = 3 + 2 * DEPTH

_INS = ["x", "c", "ctx", "c_ctx", "w_ada", "b_ada", "norm1_g", "norm2_g", "w_in", "q_norm_g", "k_norm_g", "na_rpb",
        "ret_decay", "mix_g", "w_out", "w_router", "b_router", "w_exp1", "w_exp3", "w_exp2", "final_g"]


def kernel(**inputs):
    import concourse.bacc as _bacc
    from concourse.bass_utils import run_bass_kernel_spmd as _run

    nc = _bacc.Bacc("TRN2", target_bir_lowering=False, num_devices=1)
    arrays = {f"in_{name}": np.ascontiguousarray(inputs[name]) for name in _INS}
    arrays["in_consts"], arrays["in_ids"], arrays["in_zeros"] = constants()
    g = {n[3:]: nc.dram_tensor(n, a.shape, mybir.dt.from_np(a.dtype), kind="ExternalInput").ap()
         for n, a in arrays.items()}
    out = nc.dram_tensor("out_0", (1, SEQ, D), F32, kind="ExternalOutput").ap()
    trunk(nc, g, out)
    r = _run(nc, [arrays], core_ids=[0])
    return r.results[0]["out_0"]
```
